# Optimizing a Trainium2 kernel written in Bass

```python
import math, functools
import jax, jax.numpy as jnp
from jax import lax
import numpy as np

D_MODEL = 4096
BATCH = 1
SEQ = 256
DEPTH = 1

HEAD_DIM = 128
Q_BLOCK = 128
SUPER_LEN = 1024
ROPE_THETA = 10000.0
NORM_EPS = 1e-6
SB_HEADS = 4
DSA_HEADS = 4
DSA_KV_HEADS = 1
DSA_IDX_HEADS = 4
DSA_IDX_DIM = 64
DSA_TOPK = 256
NSA_HEADS = 4
NSA_KV_HEADS = 1
NSA_CMP_LEN = 32
NSA_CMP_STRIDE = 16
NSA_SLC_LEN = 32
NSA_N_SEL = 8
NSA_WINDOW = 512
NSA_FORCED_SCORE = 1e4
DIL_PATTERNS = ((128, 1), (512, 4), (2048, 16))
DIL_GROUPS = len(DIL_PATTERNS)
DIL_HEADS_PER_GROUP = 2
DIL_MAX_WINDOW = max(w for w, _ in DIL_PATTERNS)
N_BRANCHES = 4
GATE_RANK = 256
PEER_HEADS = 8
PEER_N_KEYS = 64
PEER_EXPERTS = PEER_N_KEYS ** 2
PEER_KEY_DIM = 128
PEER_TOPK = 16

SB_W = SB_HEADS * HEAD_DIM
DSA_Q_W = DSA_HEADS * HEAD_DIM
DSA_KV_W = DSA_KV_HEADS * HEAD_DIM
DSA_IQ_W = DSA_IDX_HEADS * DSA_IDX_DIM
NSA_Q_W = NSA_HEADS * HEAD_DIM
NSA_KV_W = NSA_KV_HEADS * HEAD_DIM
DIL_Q_W = DIL_GROUPS * DIL_HEADS_PER_GROUP * HEAD_DIM
DIL_KV_W = DIL_HEADS_PER_GROUP * HEAD_DIM
IN_SPLITS = (SB_W, SB_W, SB_W,
             DSA_Q_W, DSA_KV_W, DSA_KV_W, DSA_IQ_W, DSA_IDX_DIM, DSA_IDX_HEADS,
             NSA_Q_W, NSA_KV_W, NSA_KV_W, NSA_KV_W, NSA_KV_W, NSA_KV_W, NSA_KV_W, NSA_HEADS * 3,
             DIL_Q_W, DIL_KV_W, DIL_KV_W)
IN_WIDTH = sum(IN_SPLITS)
SPLIT_OFFSETS = tuple(int(o) for o in np.cumsum(IN_SPLITS)[:-1])
BRANCH_WIDTHS = (SB_W, DSA_Q_W, NSA_Q_W, DIL_KV_W)
BRANCH_WIDTH = sum(BRANCH_WIDTHS)
BRANCH_OFFSETS = tuple(int(o) for o in np.cumsum(BRANCH_WIDTHS)[:-1])
N_QK_GAINS = 8

kernel_name = 'hybrid_sb_dsa_nsa_dilated_peer_trunk'

def rmsnorm(x, g):
    xf = x.astype(jnp.float32)
    y = xf * lax.rsqrt(jnp.mean(xf * xf, axis=-1, keepdims=True) + NORM_EPS)
    return (y * g.astype(jnp.float32)).astype(x.dtype)

def rope_tables(seq, dtype):
    inv = ROPE_THETA ** (-jnp.arange(0, HEAD_DIM, 2, dtype=jnp.float32) / HEAD_DIM)
    ang = jnp.arange(seq, dtype=jnp.float32)[:, None] * inv[None, :]
    return jnp.cos(ang)[None, :, None, :].astype(dtype), jnp.sin(ang)[None, :, None, :].astype(dtype)

def apply_rope(x, cos, sin):
    x1, x2 = jnp.split(x, 2, axis=-1)
    return jnp.concatenate([x1 * cos - x2 * sin, x2 * cos + x1 * sin], axis=-1)

def softmax_stats(s, mask):
    s = jnp.where(mask, s, -jnp.inf)
    m = jnp.max(s, axis=-1, keepdims=True)
    m = jnp.where(jnp.isfinite(m), m, 0.0)
    e = jnp.where(mask, jnp.exp(s - m), 0.0)
    return e, m, jnp.sum(e, axis=-1, keepdims=True)

def masked_softmax(s, mask):
    e, _, den = softmax_stats(s, mask)
    return e / jnp.maximum(den, jnp.finfo(jnp.float32).tiny)

def block_map(fn, n_blocks):
    out = lax.map(fn, jnp.arange(n_blocks))
    nb, b, t, f = out.shape
    return jnp.swapaxes(out, 0, 1).reshape(b, nb * t, f)

def causal_blocks(fn, seq):
    outs = []
    for start in range(0, seq, SUPER_LEN):
        stop = min(start + SUPER_LEN, seq)
        out = lax.map(lambda i: fn(start + i * Q_BLOCK, stop), jnp.arange((stop - start) // Q_BLOCK))
        nb, b, t, f = out.shape
        outs.append(jnp.swapaxes(out, 0, 1).reshape(b, nb * t, f))
    return jnp.concatenate(outs, axis=1)

def stick_breaking_attention(q, k, v):
    B, S, H, Dh = q.shape
    scale = Dh ** -0.5
    tri = jnp.tril(jnp.ones((Q_BLOCK, Q_BLOCK), jnp.float32), -1)

    def block(q0, n_keys):
        qb = lax.dynamic_slice_in_dim(q, q0, Q_BLOCK, axis=1)
        kb = k[:, :n_keys]
        vb = v[:, :n_keys]
        tpos = q0 + jnp.arange(Q_BLOCK)
        causal = (jnp.arange(n_keys)[None, :] < tpos[:, None])[None, None]
        z = jnp.einsum('bthd,bshd->bhts', qb, kb).astype(jnp.float32) * scale
        log_1m = jnp.where(causal, jax.nn.log_sigmoid(-z), 0.0)
        lm = log_1m.reshape(B, H, Q_BLOCK, n_keys // Q_BLOCK, Q_BLOCK)
        within = jnp.einsum('bhtnk,kj->bhtnj', lm, tri)
        bsum = jnp.sum(lm, axis=-1)
        later = lax.cumsum(bsum, axis=3, reverse=True) - bsum
        between = (within + later[..., None]).reshape(B, H, Q_BLOCK, n_keys)
        w = jnp.where(causal, jnp.exp(jax.nn.log_sigmoid(z) + between), 0.0)
        o = jnp.einsum('bhts,bshd->bthd', w.astype(v.dtype), vb)
        return o.reshape(B, Q_BLOCK, H * Dh)

    return causal_blocks(block, S)

def dsa_attention(q, k, v, iq, ik, iw):
    B, S, H, Dh = q.shape
    Hkv = k.shape[2]
    G = H // Hkv
    n_top = min(DSA_TOPK, S // 4)
    scale = Dh ** -0.5
    gather = jax.vmap(lambda t, idx: t[idx])

    def block(q0, n_keys):
        tpos = q0 + jnp.arange(Q_BLOCK)
        qb = lax.dynamic_slice_in_dim(q, q0, Q_BLOCK, axis=1).reshape(B, Q_BLOCK, Hkv, G, Dh)
        iqb = lax.dynamic_slice_in_dim(iq, q0, Q_BLOCK, axis=1)
        iwb = lax.dynamic_slice_in_dim(iw, q0, Q_BLOCK, axis=1).astype(jnp.float32)
        idx = jax.nn.relu(jnp.einsum('bthd,bsd->bths', iqb, ik[:, :n_keys]).astype(jnp.float32))
        idx = jnp.einsum('bths,bth->bts', idx, iwb)
        idx = jnp.where((jnp.arange(n_keys)[None, :] <= tpos[:, None])[None], idx, -jnp.inf)
        _, sel = lax.top_k(idx, n_top)
        valid = (sel <= tpos[None, :, None])[:, :, None, None, :]
        kg = gather(k, sel)
        vg = gather(v, sel)
        s = jnp.einsum('btgrd,btkgd->btgrk', qb, kg).astype(jnp.float32) * scale
        p = masked_softmax(s, valid)
        o = jnp.einsum('btgrk,btkgd->btgrd', p.astype(v.dtype), vg)
        return o.reshape(B, Q_BLOCK, H * Dh)

    return causal_blocks(block, S)

def nsa_compress(x, blk_idx, pe, w1, w2):
    blocks = x[:, blk_idx] + pe[None, None, :, None, :]
    hid = jax.nn.gelu(jnp.einsum('bnlgd,lde->bnge', blocks, w1))
    return jnp.einsum('bnge,ef->bngf', hid, w2)

def nsa_attention(q, kc, vc, ks, vs, kw, vw, gates, kc_gain, pe, w1, w2):
    B, S, H, Dh = q.shape
    Hkv = ks.shape[2]
    G = H // Hkv
    scale = Dh ** -0.5
    n_cmp = (S - NSA_CMP_LEN) // NSA_CMP_STRIDE + 1
    cmp_start = jnp.arange(n_cmp) * NSA_CMP_STRIDE
    cmp_end = cmp_start + NSA_CMP_LEN - 1
    blk_idx = cmp_start[:, None] + jnp.arange(NSA_CMP_LEN)[None, :]
    k_cmp = rmsnorm(nsa_compress(kc, blk_idx, pe[0], w1[0], w2[0]), kc_gain)
    v_cmp = nsa_compress(vc, blk_idx, pe[1], w1[1], w2[1])
    n_slc = S // NSA_SLC_LEN
    slc_start = jnp.arange(n_slc) * NSA_SLC_LEN
    overlap = ((cmp_start[:, None] < slc_start[None, :] + NSA_SLC_LEN)
               & (cmp_end[:, None] >= slc_start[None, :])).astype(jnp.float32)
    n_sel = min(NSA_N_SEL, n_slc)
    ks_t = jnp.swapaxes(ks, 1, 2)
    vs_t = jnp.swapaxes(vs, 1, 2)
    pad = ((0, 0), (NSA_WINDOW, 0), (0, 0), (0, 0))
    kw_pad = jnp.pad(kw, pad)
    vw_pad = jnp.pad(vw, pad)
    gather = jax.vmap(jax.vmap(lambda t, idx: t[idx]))

    def block(i):
        q0 = i * Q_BLOCK
        tpos = q0 + jnp.arange(Q_BLOCK)
        qb = lax.dynamic_slice_in_dim(q, q0, Q_BLOCK, axis=1).reshape(B, Q_BLOCK, Hkv, G, Dh)
        gb = lax.dynamic_slice_in_dim(gates, q0, Q_BLOCK, axis=1).reshape(B, Q_BLOCK, Hkv, G, 3)
        s_c = jnp.einsum('btgrd,bngd->btgrn', qb, k_cmp).astype(jnp.float32) * scale
        p_c = masked_softmax(s_c, (cmp_end[None, :] <= tpos[:, None])[None, :, None, None, :])
        o_c = jnp.einsum('btgrn,bngd->btgrd', p_c.astype(vc.dtype), v_cmp)
        imp = jnp.einsum('btgrn,nm->btgm', p_c, overlap)
        cur = (tpos // NSA_SLC_LEN)[:, None]
        blk = jnp.arange(n_slc)[None, :]
        forced = (blk == 0) | (blk == cur) | (blk == cur - 1)
        admissible = slc_start[None, :] <= tpos[:, None]
        imp = jnp.where(forced[None, :, None, :], NSA_FORCED_SCORE, imp)
        imp = jnp.where(admissible[None, :, None, :], imp, -jnp.inf)
        _, sel = lax.top_k(imp, n_sel)
        tok = (sel[..., None] * NSA_SLC_LEN + jnp.arange(NSA_SLC_LEN)).reshape(
            B, Q_BLOCK, Hkv, n_sel * NSA_SLC_LEN)
        tok_t = jnp.swapaxes(tok, 1, 2)
        kg = gather(ks_t, tok_t)
        vg = gather(vs_t, tok_t)
        s_s = jnp.einsum('btgrd,bgtkd->btgrk', qb, kg).astype(jnp.float32) * scale
        p_s = masked_softmax(s_s, (tok <= tpos[None, :, None, None])[:, :, :, None, :])
        o_s = jnp.einsum('btgrk,bgtkd->btgrd', p_s.astype(vs.dtype), vg)
        wpos = q0 - NSA_WINDOW + jnp.arange(NSA_WINDOW + Q_BLOCK)
        kwb = lax.dynamic_slice_in_dim(kw_pad, q0, NSA_WINDOW + Q_BLOCK, axis=1)
        vwb = lax.dynamic_slice_in_dim(vw_pad, q0, NSA_WINDOW + Q_BLOCK, axis=1)
        dist = tpos[:, None] - wpos[None, :]
        mask_w = (dist >= 0) & (dist < NSA_WINDOW) & (wpos[None, :] >= 0)
        s_w = jnp.einsum('btgrd,bjgd->btgrj', qb, kwb).astype(jnp.float32) * scale
        p_w = masked_softmax(s_w, mask_w[None, :, None, None, :])
        o_w = jnp.einsum('btgrj,bjgd->btgrd', p_w.astype(vw.dtype), vwb)
        o = gb[..., 0:1] * o_c + gb[..., 1:2] * o_s + gb[..., 2:3] * o_w
        return o.reshape(B, Q_BLOCK, H * Dh)

    return block_map(block, S // Q_BLOCK)

def dilated_attention(q, k, v):
    B, S, NG, Hs, Dh = q.shape
    scale = Dh ** -0.5
    pad = ((0, 0), (DIL_MAX_WINDOW, 0), (0, 0), (0, 0))
    k_pad = jnp.pad(k, pad)
    v_pad = jnp.pad(v, pad)

    def to_tokens(a):
        return jnp.transpose(a[..., 0], (0, 3, 2, 1)).reshape(B, Q_BLOCK, Hs)[..., None]

    def block(i):
        q0 = i * Q_BLOCK
        qb = lax.dynamic_slice_in_dim(q, q0, Q_BLOCK, axis=1)
        nums, maxes, dens = [], [], []
        for g, (window, dilation) in enumerate(DIL_PATTERNS):
            n_q = Q_BLOCK // dilation
            n_k = (window + Q_BLOCK) // dilation
            start = q0 + DIL_MAX_WINDOW - window
            kb = lax.dynamic_slice_in_dim(k_pad, start, window + Q_BLOCK, axis=1).reshape(B, n_k, dilation, Hs, Dh)
            vb = lax.dynamic_slice_in_dim(v_pad, start, window + Q_BLOCK, axis=1).reshape(B, n_k, dilation, Hs, Dh)
            qr = qb[:, :, g].reshape(B, n_q, dilation, Hs, Dh)
            ii = jnp.arange(n_q)[:, None]
            jj = jnp.arange(n_k)[None, :]
            kpos = q0 - window + jj[None] * dilation + jnp.arange(dilation)[:, None, None]
            mask = ((jj >= ii) & (jj <= ii + window // dilation))[None] & (kpos >= 0)
            s = jnp.einsum('bicsd,bjcsd->bscij', qr, kb).astype(jnp.float32) * scale
            e, m, den = softmax_stats(s, mask[None, None])
            num = jnp.einsum('bscij,bjcsd->bicsd', e, vb.astype(jnp.float32)).reshape(B, Q_BLOCK, Hs, Dh)
            nums.append(num)
            maxes.append(to_tokens(m))
            dens.append(to_tokens(den))
        m_all = functools.reduce(jnp.maximum, maxes)
        wts = [jnp.exp(m - m_all) for m in maxes]
        num = functools.reduce(jnp.add, [w * n for w, n in zip(wts, nums)])
        den = functools.reduce(jnp.add, [w * d for w, d in zip(wts, dens)])
        o = (num / den).astype(v.dtype)
        return o.reshape(B, Q_BLOCK, Hs * Dh)

    return block_map(block, S // Q_BLOCK)

def token_mixing(xn, cos, sin, w_in, qk_gain, nsa_pe, nsa_w1, nsa_w2, gate_down, gate_up, w_branch, w_out):
    B, S, _ = xn.shape
    (a_q, a_k, a_v, b_q, b_k, b_v, b_iq, b_ik, b_iw,
     c_q, c_kc, c_vc, c_ks, c_vs, c_kw, c_vw, c_g,
     d_q, d_k, d_v) = jnp.split(xn @ w_in, SPLIT_OFFSETS, axis=-1)

    def heads(t, n):
        return t.reshape(B, S, n, -1)

    def qk(t, n, gi):
        return apply_rope(rmsnorm(heads(t, n), qk_gain[gi]), cos, sin)

    o_a = stick_breaking_attention(heads(a_q, SB_HEADS), heads(a_k, SB_HEADS), heads(a_v, SB_HEADS))
    o_b = dsa_attention(qk(b_q, DSA_HEADS, 0), qk(b_k, DSA_KV_HEADS, 1), heads(b_v, DSA_KV_HEADS),
                        heads(b_iq, DSA_IDX_HEADS), b_ik, b_iw)
    o_c = nsa_attention(qk(c_q, NSA_HEADS, 2),
                        apply_rope(heads(c_kc, NSA_KV_HEADS), cos, sin), heads(c_vc, NSA_KV_HEADS),
                        qk(c_ks, NSA_KV_HEADS, 4), heads(c_vs, NSA_KV_HEADS),
                        qk(c_kw, NSA_KV_HEADS, 5), heads(c_vw, NSA_KV_HEADS),
                        jax.nn.sigmoid(c_g).reshape(B, S, NSA_HEADS, 3),
                        qk_gain[3], nsa_pe, nsa_w1, nsa_w2)
    dq = qk(d_q, DIL_GROUPS * DIL_HEADS_PER_GROUP, 6).reshape(B, S, DIL_GROUPS, DIL_HEADS_PER_GROUP, HEAD_DIM)
    o_d = dilated_attention(dq, qk(d_k, DIL_HEADS_PER_GROUP, 7), heads(d_v, DIL_HEADS_PER_GROUP))

    z = xn @ gate_down
    merged = None
    for i, (o, wb) in enumerate(zip((o_a, o_b, o_c, o_d), jnp.split(w_branch, BRANCH_OFFSETS, axis=0))):
        gate = jax.nn.sigmoid((z @ gate_up[i]).astype(jnp.float32)).astype(xn.dtype)
        term = gate * (o @ wb)
        merged = term if merged is None else merged + term
    return merged @ w_out

def peer_ffn(xn, wq, subkeys, u, v):
    B, S, _ = xn.shape
    q = (xn @ wq).reshape(B, S, PEER_HEADS, PEER_KEY_DIM)
    q1, q2 = jnp.split(q, 2, axis=-1)
    s1 = jnp.einsum('bshd,hnd->bshn', q1, subkeys[:, 0]).astype(jnp.float32)
    s2 = jnp.einsum('bshd,hnd->bshn', q2, subkeys[:, 1]).astype(jnp.float32)
    v1, i1 = lax.top_k(s1, PEER_TOPK)
    v2, i2 = lax.top_k(s2, PEER_TOPK)
    cand_s = (v1[..., :, None] + v2[..., None, :]).reshape(B, S, PEER_HEADS, PEER_TOPK * PEER_TOPK)
    cand_e = (i1[..., :, None] * PEER_N_KEYS + i2[..., None, :]).reshape(B, S, PEER_HEADS, PEER_TOPK * PEER_TOPK)
    top_s, top_pos = lax.top_k(cand_s, PEER_TOPK)
    experts = jnp.take_along_axis(cand_e, top_pos, axis=-1).reshape(B * S, PEER_HEADS * PEER_TOPK)
    gates = jax.nn.softmax(top_s, axis=-1).reshape(B * S, PEER_HEADS * PEER_TOPK)
    act = jax.nn.gelu(jnp.einsum('bsd,ed->bse', xn, u).astype(jnp.float32)).reshape(B * S, PEER_EXPERTS)
    coef = gates * jnp.take_along_axis(act, experts, axis=-1)
    wmat = jnp.zeros((B * S, PEER_EXPERTS), jnp.float32).at[jnp.arange(B * S)[:, None], experts].add(coef)
    return (wmat.astype(v.dtype) @ v).reshape(B, S, -1)

def setup_inputs(seed: int = 0) -> dict:
    key = jax.random.key(seed)
    ks = jax.random.split(key, 16)

    def nrm(k, shape, scale):
        return jax.random.normal(k, shape, jnp.float32) * scale

    return {
        'x': nrm(ks[0], (BATCH, SEQ, D_MODEL), 1.0),
        'norm_mix': 1.0 + nrm(ks[1], (DEPTH, D_MODEL), 0.02),
        'w_in': nrm(ks[2], (DEPTH, D_MODEL, IN_WIDTH), D_MODEL ** -0.5),
        'qk_gain': 1.0 + nrm(ks[3], (DEPTH, N_QK_GAINS, HEAD_DIM), 0.02),
        'nsa_pe': nrm(ks[4], (DEPTH, 2, NSA_CMP_LEN, HEAD_DIM), 0.1),
        'nsa_w1': nrm(ks[5], (DEPTH, 2, NSA_CMP_LEN, HEAD_DIM, HEAD_DIM), (NSA_CMP_LEN * HEAD_DIM) ** -0.5),
        'nsa_w2': nrm(ks[6], (DEPTH, 2, HEAD_DIM, HEAD_DIM), HEAD_DIM ** -0.5),
        'gate_down': nrm(ks[7], (DEPTH, D_MODEL, GATE_RANK), D_MODEL ** -0.5),
        'gate_up': nrm(ks[8], (DEPTH, N_BRANCHES, GATE_RANK, D_MODEL), GATE_RANK ** -0.5),
        'w_branch': nrm(ks[9], (DEPTH, BRANCH_WIDTH, D_MODEL), SB_W ** -0.5),
        'w_out': nrm(ks[10], (DEPTH, D_MODEL, D_MODEL), D_MODEL ** -0.5),
        'norm_ffn': 1.0 + nrm(ks[11], (DEPTH, D_MODEL), 0.02),
        'peer_wq': nrm(ks[12], (DEPTH, D_MODEL, PEER_HEADS * PEER_KEY_DIM), D_MODEL ** -0.5),
        'peer_subkeys': nrm(ks[13], (DEPTH, PEER_HEADS, 2, PEER_N_KEYS, PEER_KEY_DIM // 2), (PEER_KEY_DIM // 2) ** -0.5),
        'peer_u': nrm(ks[14], (DEPTH, PEER_EXPERTS, D_MODEL), D_MODEL ** -0.5),
        'peer_v': nrm(ks[15], (DEPTH, PEER_EXPERTS, D_MODEL), (PEER_HEADS * PEER_TOPK) ** -0.5),
    }

def reference(x, norm_mix, w_in, qk_gain, nsa_pe, nsa_w1, nsa_w2, gate_down, gate_up, w_branch, w_out,
              norm_ffn, peer_wq, peer_subkeys, peer_u, peer_v):
    cos, sin = rope_tables(x.shape[1], x.dtype)
    h = x
    for l in range(DEPTH):
        xn = rmsnorm(h, norm_mix[l])
        h = h + token_mixing(xn, cos, sin, w_in[l], qk_gain[l], nsa_pe[l], nsa_w1[l], nsa_w2[l],
                             gate_down[l], gate_up[l], w_branch[l], w_out[l])
        h = h + peer_ffn(rmsnorm(h, norm_ffn[l]), peer_wq[l], peer_subkeys[l], peer_u[l], peer_v[l])
    return h


_drawn_inputs = setup_inputs


def setup_inputs(seed=0):
    import zlib

    import numpy as np

    out = dict(_drawn_inputs(seed))
    spreads = {}
    factors = {'norm_mix': 3.2, 'qk_gain': 8.0, 'nsa_pe': 3.708, 'norm_ffn': 23.199}
    for name, (base, spread) in spreads.items():
        noise = np.random.default_rng([zlib.crc32(name.encode()), seed]).standard_normal(out[name].shape)
        drawn = base * np.exp(spread * noise) if base else spread * noise
        out[name] = __import__('jax').numpy.asarray(drawn.astype(out[name].dtype))
    for name, factor in factors.items():
        out[name] = (out[name] * factor).astype(out[name].dtype)
    return out
```

```python
import numpy as np

import concourse.bass as bass
from concourse import mybir

F32 = mybir.dt.float32
F32R = mybir.dt.float32r
BF16 = mybir.dt.bfloat16
U32 = mybir.dt.uint32
ALU = mybir.AluOpType
ACT = mybir.ActivationFunctionType
AX = mybir.AxisListType.X

P = 128
S = 256
NT = S // P
D = 4096
KT = D // P
HD = 128
EPS = 1e-6
SCALE = HD ** -0.5
NEG = -1e38
TAKEN = -3e38
TINY = float(np.finfo(np.float32).tiny)

NORMED = 19
ROPED = 20
(H_BQ, H_BK, H_CQ, H_CKS, H_CKW, H_DQ, H_DK, H_CKC, H_CVC) = (0, 4, 5, 9, 10, 11, 17, 19, 20)
GAIN_SPANS = ((0, 4, 0), (4, 5, 1), (5, 9, 2), (9, 10, 4), (10, 11, 5), (11, 17, 6), (17, 19, 7))
C_IQ = 21 * HD
C_IK = C_IQ + 256
C_IW = C_IK + 64
C_BV = C_IW + 4
C_CVS = C_BV + HD
C_CVW = C_CVS + HD
C_DV = C_CVW + HD
C_CG = C_DV + 2 * HD
C_AQ = C_CG + 12
C_AV = C_AQ + 8 * HD
C_Z = C_AV + 4 * HD
NCOL = C_Z + 256
NG1 = 11
W1C = NCOL // NG1
assert NG1 * W1C == NCOL and W1C <= 512
T_AQ, T_AK = 21, 25
NTB = 29

RING = 4
CPG = KT // 2
GRP = D // 512
G_IN, G_MIX, G_OUT, G_WQ, G_U, G_V = NG1, 8 * GRP, GRP, 2, GRP, GRP
BRANCHES = ((0, 4), (4, 4), (8, 4), (12, 2))
CH_IN = 0
CH_MIX = CH_IN + NG1 * CPG
CH_OUT = CH_MIX + sum(GRP * (1 + n // 2) for _, n in BRANCHES)
CH_WQ = CH_OUT + GRP * CPG
CH_U = CH_WQ + 2 * CPG
CH_V = CH_U + GRP * CPG
CH_END = CH_V + GRP * CPG
GN_IN = 0
GN_MIX = GN_IN + G_IN
GN_OUT = GN_MIX + G_MIX
GN_WQ = GN_OUT + G_OUT
GN_U = GN_WQ + G_WQ
GN_V = GN_U + G_U

NCMP = (S - 32) // 16 + 1
PH, PK = 8, 16
KB = 1024


def build(nc, io):
    base = (nc.sbuf_base + 31) // 32 * 32
    XT0 = base
    RG0 = XT0 + 64 * KB
    MG0 = RG0 + 12 * RING * KB
    PJ0 = MG0 + 32 * KB
    CN0 = PJ0 + NT * NCOL * 4

    def at(name, shape, dt, off):
        return nc.alloc_sbuf_tensor_at(name, shape, dt, offset=off)

    cursor = [CN0]

    def const(name, shape, dt=F32):
        n = int(np.prod(shape[1:])) * (2 if dt == BF16 else 4)
        t = at(name, shape, dt, cursor[0])
        cursor[0] += (n + 31) // 32 * 32
        return t

    xt_hi = at("xt_hi", [P, KT, S], F32R, XT0)
    xt_lo = at("xt_lo", [P, KT, S], F32R, XT0 + 32 * KB)
    w_raw = at("w_raw", [P, RING, 1024], F32, RG0)
    w_hi = at("w_hi", [P, RING, 1024], F32R, RG0 + 4 * RING * KB)
    w_lo = at("w_lo", [P, RING, 1024], F32R, RG0 + 8 * RING * KB)
    xt_raw = at("xt_raw", [P, KT, S], F32, MG0)
    rows = at("rows", [P, NT, D], F32, MG0)
    cmp_w1 = at("cmp_w1", [P, 32, P], F32, MG0)
    rope_tmp = at("rope_tmp", [P, ROPED * HD], F32, MG0 + 16 * KB)
    gains = at("gains", [P, 8, HD], F32, MG0 + 28 * KB)
    probs = at("probs", [P, 6, S], F32, MG0 + 16 * KB)
    probs_t = at("probs_t", [P, 2, 4, P], F32, MG0 + 22 * KB)
    idx_tmp = at("idx_tmp", [P, S], F32, MG0 + 26 * KB)
    idx_sum = at("idx_sum", [P, S], F32, MG0 + 27 * KB)
    sel_mask = at("sel_mask", [P, NT, S], F32, MG0 + 28 * KB)
    stick_z = at("stick_z", [P, 2, 2, S], F32, MG0)
    stick_e = at("stick_e", [P, 2, 2, S], F32, MG0 + 4 * KB)
    stick_l = at("stick_l", [P, 2, 2, S], F32, MG0 + 8 * KB)
    proj = at("proj", [P, NT, NCOL], F32, PJ0)
    zt_hi = at("zt_hi", [P, 2, S], F32R, PJ0)
    zt_lo = at("zt_lo", [P, 2, S], F32R, PJ0 + 2 * KB)
    gate = at("gate", [P, 2, NT, 512], F32, PJ0 + 8 * KB)
    peer_q = at("peer_q", [P, NT, PH * HD], F32, PJ0)
    peer_qt = at("peer_qt", [P, PH, S], F32, PJ0 + 8 * KB)
    subkeys = at("subkeys", [P, PH, P], F32, PJ0 + 16 * KB)
    square = at("square", [P, D], F32, PJ0 + 20 * KB)
    act_rows = at("act_rows", [P, NT, D], F32, PJ0)
    key_s = at("key_s", [P, NT, PH, 2, 64], F32, PJ0 + 32 * KB)
    feat = at("feat", [P, NTB, S], F32, XT0)
    idx_t = at("idx_t", [64, 5, S], F32, XT0 + 29 * KB)
    ot_hi = at("ot_hi", [P, 14, S], F32R, XT0 + 34 * KB)
    ot_lo = at("ot_lo", [P, 14, S], F32R, XT0 + 48 * KB)
    act_t = at("act_t", [P, KT, S], F32, XT0 + 32 * KB)
    hot_c = at("hot_c", [P, 16, P], BF16, PJ0)
    hot_q = at("hot_q", [P, 32, 32], F32, PJ0 + 4 * KB)
    hot_g = at("hot_g", [P, 3, 32, 32], BF16, PJ0 + 8 * KB)
    wmat = at("wmat", [P, KT, 16], F32, PJ0 + 16 * KB)

    kmaj = at("kmaj", [P, 3, S], F32, PJ0 + 32 * KB)
    g_parts = at("g_parts", [P, 5, S], F32, PJ0 + 35 * KB)

    ident = const("ident", [P, P])
    g_mix = const("g_mix", [P, KT])
    g_ffn = const("g_ffn", [P, KT])
    iotas = const("iotas", [P, P])
    small = const("small", [P, 256])
    tail0 = cursor[0]
    causal = const("causal", [P, NT, S])
    dil = const("dil", [P, NT, 3, S])
    strict = const("strict", [P, 2, S])
    rope = const("rope", [P, 3, NT, 64])
    tri = const("tri", [P, 2, P])
    cmp_mask = const("cmp_mask", [P, NT, NCMP])
    pe_t = const("pe_t", [P, 2, 32])
    cmp_w2 = const("cmp_w2", [P, 2, P])
    cmp_b = at("cmp_b", [P, 32, NCMP], F32, MG0 + 16 * KB)
    cmp_h = const("cmp_h", [P, 2, NCMP])
    k_cmp = const("k_cmp", [NCMP, HD])
    k_sq = const("k_sq", [NCMP, HD])
    v_cmp = const("v_cmp", [NCMP, HD])
    gains_cmp = const("gains_cmp", [NCMP, HD])
    kt_cmp = const("kt_cmp", [P, NCMP])
    assert cursor[0] <= nc.sbuf_usable_end
    cursor[0] = tail0
    key_v = const("key_v", [P, NT, PH, 2, PK])
    key_i = const("key_i", [P, NT, PH, 2, PK], U32)
    pair_v = const("pair_v", [P, NT, PH, PK])
    pair_i = const("pair_i", [P, NT, PH, PK], U32)
    cand = const("cand", [P, PK, PK])
    key_w = const("key_w", [P, 64])
    key_f = const("key_f", [P, 2, PK])
    pair_n = const("pair_n", [P, 2, PK], U32)
    pair_f = const("pair_f", [P, 2, PK])
    picks = const("picks", [P, NT, 3, PH, PK])
    pick_n = const("pick_n", [P, 2, PK], U32)
    assert cursor[0] <= nc.sbuf_usable_end

    rstd_x = small[:, 0:2]
    ms_x = small[:, 2:4]
    ms_h = small[:, 4:6]
    rstd_h = small[:, 6:8]
    head_ms = small[:, 8:28]
    head_rstd = small[:, 28:48]
    half_exp = small[:, 48:68]
    row_max = small[:, 68:74]
    row_neg = small[:, 74:80]
    row_den = small[:, 80:86]
    row_inv = small[:, 86:92]
    nsa_gate = small[:, 92:116]
    top8 = small[:, 116:124]
    k_ms = small[0:NCMP, 124:125]
    k_rstd = small[0:NCMP, 125:126]
    soft_den = small[:, 128:144]
    soft_inv = small[:, 144:160]

    acc = nc.alloc_psum_tensor("acc", [P, 2, NT, 512], F32)
    side = nc.alloc_psum_tensor("side", [P, 4, 512], F32)

    cmp_outs = (side[0:NCMP, 3, 0:HD], acc[0:NCMP, 0, 0, 0:HD])

    def sem(name):
        return nc.alloc_semaphore(name)

    raw_loaded = [sem(f"raw_loaded{i}") for i in range(RING)]
    hi_ready, lo_ready, chunk_used = sem("hi_ready"), sem("lo_ready"), sem("chunk_used")
    bank_free = [sem("bank_free0"), sem("bank_free1")]
    xt_loaded, const_loaded, attn_loaded = sem("xt_loaded"), sem("const_loaded"), sem("attn_loaded")
    rows_loaded, cmp_loaded, cmp_loaded2 = sem("rows_loaded"), sem("cmp_loaded"), sem("cmp_loaded2")
    gains_loaded = sem("gains_loaded")
    subkeys_loaded = sem("subkeys_loaded")
    xt_hi_done, xt_lo_done, xt_turned = sem("xt_hi_done"), sem("xt_lo_done"), sem("xt_turned")
    squares_done, rstd_ready = sem("squares_done"), sem("rstd_ready")
    head_ms_done, head_rstd_done, heads_ready = sem("head_ms_done"), sem("head_rstd_done"), sem("heads_ready")
    turned, turned_copied = sem("turned"), sem("turned_copied")
    z_turned, z_hi_done, z_lo_done = sem("z_turned"), sem("z_hi_done"), sem("z_lo_done")
    index_ready, index_read, index_selected = sem("index_ready"), sem("index_read"), sem("index_selected")
    scores_ready, row_max_ready, exp_ready = sem("scores_ready"), sem("row_max_ready"), sem("exp_ready")
    probs_ready, probs_turned, probs_copied = sem("probs_ready"), sem("probs_turned"), sem("probs_copied")
    pv_done, out_hi_done, out_lo_done = sem("pv_done"), sem("out_hi_done"), sem("out_lo_done")
    cmp_blocks, cmp_hidden, cmp_act = sem("cmp_blocks"), sem("cmp_hidden"), sem("cmp_act")
    cmp_out, cmp_kept, cmp_square, cmp_rstd = sem("cmp_out"), sem("cmp_kept"), sem("cmp_square"), sem("cmp_rstd")
    cmp_normed, cmp_turned, cmp_ready = sem("cmp_normed"), sem("cmp_turned"), sem("cmp_ready")
    nsa_gate_ready = sem("nsa_gate_ready")
    stick_scores, stick_soft, stick_masked = sem("stick_scores"), sem("stick_soft"), sem("stick_masked")
    stick_sums, stick_arg, stick_exp = sem("stick_sums"), sem("stick_arg"), sem("stick_exp")
    stick_weights, stick_out = sem("stick_weights"), sem("stick_out")
    stick_hi, stick_lo = sem("stick_hi"), sem("stick_lo")
    gate_used = sem("gate_used")
    pq_turned, pq_copied = sem("pq_turned"), sem("pq_copied")
    key_scores, key_copied = sem("key_scores"), sem("key_copied")
    picks_shifted, picks_exp, picks_ready = sem("picks_shifted"), sem("picks_exp"), sem("picks_ready")
    picks_turned, picks_copied = sem("picks_turned"), sem("picks_copied")
    act_turned, act_copied = sem("act_turned"), sem("act_copied")
    hot_ready, scattered, wmat_ready, wmat_hi, wmat_lo = (
        sem("hot_ready"), sem("scattered"), sem("wmat_ready"), sem("wmat_hi"), sem("wmat_lo"))
    stored, gain_cmp_loaded = sem("stored"), sem("gain_cmp_loaded")
    dve_chain, act_chain, pool_chain = sem("dve_chain"), sem("act_chain"), sem("pool_chain")

    def chain(eng, own):
        count = [0]

        def then(instruction):
            count[0] += 1
            instruction.then_inc(own, 1)
            eng.wait_ge(own, count[0])
        return then

    def tile_rows(h):
        return slice(h * P, (h + 1) * P)

    passes = [("b", 0, 0), ("b", 1, 0),
              ("c", 0, 0), ("c", 0, 1), ("c", 0, 2), ("c", 1, 0), ("c", 1, 1), ("c", 1, 2),
              ("d", 0, 0), ("d", 1, 0)]
    ot_block = {"b": 0, "c": 4, "a": 8, "d": 12}

    def last_of_output(br, part):
        return br != "c" or part == 2

    mix_chunk, c0 = [], CH_MIX
    for _, n in BRANCHES:
        mix_chunk.append(c0)
        c0 += GRP * (1 + n // 2)

    with nc.Block() as block:

        @block.sync
        def _(sp):
            def load(src, slot, width, used_by=None):
                if used_by is not None:
                    sp.wait_ge(lo_ready, used_by)
                sp.dma_start(w_raw[:, slot, 0:width], src).then_inc(raw_loaded[slot], 16)

            for c in range(RING):
                load(io["w_in"][c], c, 2 * W1C)
            with sp.Fori(1, NG1 * CPG // RING) as g:
                for c in range(RING):
                    load(io["w_in"][bass.ds(g * RING + c, 1)].rearrange("a p n -> (a p) n"), c, 2 * W1C,
                         g * RING + (c - RING + 1))
            n_in = NG1 * CPG
            with sp.Fori(0, (CH_END - n_in) // RING) as g:
                for c in range(RING):
                    load(io["stream"][bass.ds(g * RING + c, 1)].rearrange("a p n -> (a p) n"), c, 1024,
                         g * RING + (n_in + c - RING + 1))

        @block.tensor
        def _(pe):
            def products(parity, chunk, slot, lhs_hi, lhs_lo, k0, width, first, last):
                pe.wait_ge(lo_ready, chunk + 1)
                for j in range(2):
                    wh = w_hi[:, slot, j * width:(j + 1) * width]
                    wl = w_lo[:, slot, j * width:(j + 1) * width]
                    for h in range(NT):
                        o = acc[:, parity, h, 0:width]
                        xh = lhs_hi[:, k0 + j, tile_rows(h)]
                        xl = lhs_lo[:, k0 + j, tile_rows(h)]
                        pe.matmul(o, xh, wh, start=first and j == 0, stop=False)
                        pe.matmul(o, xh, wl, start=False, stop=False)
                        mm = pe.matmul(o, xl, wh, start=False, stop=last and j == 1)
                mm.then_inc(chunk_used, 1)

            def bank(parity, uses):
                if not (isinstance(uses, int) and uses == 0):
                    pe.wait_ge(bank_free[parity], uses)

            def full_group(gn, chunk, lhs_hi, lhs_lo, width, uses):
                parity = gn % 2
                bank(parity, uses)
                for c in range(CPG):
                    products(parity, chunk + c, c % RING, lhs_hi, lhs_lo, 2 * c, width, c == 0, c == CPG - 1)

            bank(0, 0)
            for c in range(CPG):
                pe.wait_ge(xt_lo_done, 2 * c + 2)
                products(0, c, c % RING, xt_hi, xt_lo, 2 * c, W1C, c == 0, c == CPG - 1)
            full_group(1, CPG, xt_hi, xt_lo, W1C, 0)
            with pe.Fori(1, 5) as i:
                for g in range(2):
                    full_group(g, i * (2 * CPG) + g * CPG, xt_hi, xt_lo, W1C, i)
            full_group(0, 10 * CPG, xt_hi, xt_lo, W1C, 5)

            pe.wait_ge(heads_ready, NT)
            blocks = [b for b in range(NTB)]
            cols = [b * HD if b < 21 else C_AQ + (b - 21) * HD for b in blocks]
            for n in range(0, 30, 2):
                if n // 2 >= 4:
                    pe.wait_ge(turned_copied, n // 2 - 3)
                for b in range(n, min(n + 2, NTB)):
                    for h in range(NT):
                        mm = pe.transpose(side[:, n // 2 % 4, (b - n) * S + h * P:(b - n) * S + (h + 1) * P],
                                          proj[:, h, cols[b]:cols[b] + HD], ident[:])
                mm.then_inc(turned, 1)
            for n in range(3):
                pe.wait_ge(turned_copied, 15 + n - 3)
                for b in range(2 * n, min(2 * n + 2, 5)):
                    for h in range(NT):
                        mm = pe.transpose(side[0:64, (15 + n) % 4, (b - 2 * n) * S + h * P:(b - 2 * n) * S + (h + 1) * P],
                                          proj[:, h, C_IQ + 64 * b:C_IQ + 64 * b + 64], ident[:])
                mm.then_inc(turned, 1)
            pe.wait_ge(turned_copied, 15)
            for b in range(2):
                for h in range(NT):
                    mm = pe.transpose(side[:, 18 % 4, b * S + h * P:b * S + (h + 1) * P],
                                      proj[:, h, C_Z + b * P:C_Z + (b + 1) * P], ident[:])
            mm.then_inc(z_turned, 1)
            pe.wait_ge(turned_copied, 18)
            pe.wait_ge(z_lo_done, 1)

            for h in range(NT):
                if h:
                    pe.wait_ge(index_read, h)
                for i in range(4):
                    mm = pe.matmul(side[:, i // 2, (i % 2) * S:(i % 2 + 1) * S],
                                   idx_t[:, i, tile_rows(h)], idx_t[:, 4, :], start=True, stop=True)
                mm.then_inc(index_ready, 1)

            for w in range(2):
                pe.wait_ge(cmp_loaded if w == 0 else cmp_loaded2, 16)
                pe.wait_ge(cmp_blocks, w + 1)
                for l in range(32):
                    mm = pe.matmul(side[:, 2, w * 32:w * 32 + NCMP], cmp_w1[:, l, :], cmp_b[:, l, :],
                                   start=(l == 0), stop=(l == 31))
                mm.then_inc(cmp_hidden, 1)
                pe.wait_ge(cmp_act, w + 1)
                pe.matmul(cmp_outs[w], cmp_h[:, w, :], cmp_w2[:, w, :],
                          start=True, stop=True).then_inc(cmp_out, 1)
            pe.wait_ge(cmp_normed, 1)
            pe.transpose(side[:, 2, 64:64 + NCMP], k_cmp[:], ident[0:NCMP, 0:NCMP]).then_inc(cmp_turned, 1)
            pe.wait_ge(cmp_ready, 1)
            pe.wait_ge(index_read, 2)

            n_out = 0
            for i, (br, h, part) in enumerate(passes):
                if i:
                    pe.wait_ge(probs_copied, i)
                t = tile_rows(h)
                if br == "b":
                    pairs = [(H_BQ + r, feat[:, H_BK, :]) for r in range(4)]
                elif br == "c":
                    key = (kt_cmp[:], feat[:, H_CKS, :], feat[:, H_CKW, :])[part]
                    pairs = [(H_CQ + r, key) for r in range(4)]
                else:
                    pairs = [(H_DQ + 2 * g + s, feat[:, H_DK + s, :]) for s in range(2) for g in range(3)]
                nk = NCMP if (br, part) == ("c", 0) else S
                for r, (q, key) in enumerate(pairs):
                    mm = pe.matmul(side[:, r // 2, (r % 2) * S:(r % 2) * S + nk], feat[:, q, t], key,
                                   start=True, stop=True)
                mm.then_inc(scores_ready, 1)
                pe.wait_ge(probs_ready, i + 1)
                heads = 2 if br == "d" else 4
                for s in range(1 if nk == NCMP else 2):
                    for r in range(heads):
                        mm = pe.transpose(side[0:min(nk, P), s, r * P:(r + 1) * P],
                                          probs[:, 3 * r if br == "d" else r, s * P:min((s + 1) * P, nk)], ident[:])
                mm.then_inc(probs_turned, 1)
                pe.wait_ge(probs_copied, i + 1)
                if (br == "c" and part == 0) or br != "c":
                    if n_out:
                        pe.wait_ge(out_lo_done, n_out)
                if nk == NCMP:
                    mm = pe.matmul(side[:, 3, :], v_cmp[:], probs_t[0:NCMP, 0, :, :], start=True, stop=False)
                elif br == "d":
                    for hs in range(2):
                        for s in range(2):
                            mm = pe.matmul(side[:, 3, hs * P:(hs + 1) * P],
                                           proj[:, s, C_DV + hs * HD:C_DV + (hs + 1) * HD],
                                           probs_t[:, s, hs, :], start=(s == 0), stop=(s == 1))
                else:
                    col = {("b", 0): C_BV, ("c", 1): C_CVS, ("c", 2): C_CVW}[br, part]
                    for s in range(2):
                        mm = pe.matmul(side[:, 3, :], proj[:, s, col:col + HD], probs_t[:, s, :, :],
                                       start=(s == 0 and br == "b"), stop=(s == 1 and last_of_output(br, part)))
                mm.then_inc(pv_done, 1)
                if last_of_output(br, part):
                    n_out += 1

            pe.wait_ge(probs_copied, len(passes))
            pe.wait_ge(out_lo_done, n_out)
            for u in range(2):
                if u:
                    pe.wait_ge(stick_lo, 1)
                for r in range(2):
                    for s in range(2):
                        mm = pe.matmul(side[:, r, s * S:(s + 1) * S],
                                       feat[:, T_AK + 2 * u + r, tile_rows(s)], feat[:, T_AQ + 2 * u + r, :],
                                       start=True, stop=True)
                mm.then_inc(stick_scores, 1)
                pe.wait_ge(stick_masked, u + 1)
                for r in range(2):
                    pe.matmul(side[:, 2 + r, 0:S], tri[:, 0, :], stick_l[:, r, 0, :], start=True, stop=False)
                    pe.matmul(side[:, 2 + r, 0:S], tri[:, 1, :], stick_l[:, r, 1, :], start=False, stop=True)
                    mm = pe.matmul(side[:, 2 + r, S:2 * S], tri[:, 0, :], stick_l[:, r, 1, :], start=True, stop=True)
                mm.then_inc(stick_sums, 1)
                pe.wait_ge(stick_weights, u + 1)
                for r in range(2):
                    for s in range(2):
                        col = C_AV + (2 * u + r) * HD
                        mm = pe.matmul(side[:, 0, r * S:(r + 1) * S], proj[:, s, col:col + HD],
                                       stick_e[:, r, s, :], start=(s == 0), stop=(s == 1))
                mm.then_inc(stick_out, 1)

            pe.wait_ge(stick_lo, 2)
            for i, (b0, n) in enumerate(BRANCHES):
                per = 1 + n // 2
                pairs_before = GN_MIX // 2

                def mix_group(m, k, uses):
                    c = mix_chunk[i] + m * per
                    slot = (mix_chunk[i] + k * per) % RING
                    bank(1, uses)
                    products(1, c, slot, zt_hi, zt_lo, 0, 512, True, True)
                    bank(0, uses + 1)
                    for j in range(n // 2):
                        products(0, c + 1 + j, (slot + 1 + j) % RING, ot_hi, ot_lo, b0 + 2 * j, 512,
                                 j == 0, j == n // 2 - 1)
                with pe.Fori(0, GRP // 4) as m:
                    for k in range(4):
                        mix_group(m * 4 + k, k, m * 4 + (k + i * GRP + pairs_before))

            def turn_rows(count0, ready):
                for q in range(KT // 2):
                    if q == 0:
                        ready()
                    if count0 + q >= 4:
                        pe.wait_ge(xt_lo_done, KT + count0 + q - 3)
                    for j in range(2):
                        for h in range(NT):
                            mm = pe.transpose(side[:, q % 4, j * S + h * P:j * S + (h + 1) * P],
                                              rows[:, h, (2 * q + j) * P:(2 * q + j + 1) * P], ident[:])
                    mm.then_inc(xt_turned, 1)

            def groups(gn0, ch0, n, lhs_hi, lhs_lo):
                with pe.Fori(0, n // 2) as m:
                    for k in range(2):
                        gn = gn0 + k
                        full_group(gn, m * (2 * CPG) + (ch0 + k * CPG), lhs_hi, lhs_lo, 512, m + gn // 2)

            def all_free(gn_next):
                pe.wait_ge(bank_free[gn_next % 2], gn_next // 2)
                pe.wait_ge(bank_free[(gn_next + 1) % 2], (gn_next + 1) // 2)

            turn_rows(0, lambda: pe.wait_ge(gate_used, 4 * GRP))
            pe.wait_ge(xt_lo_done, KT + KT // 2)
            groups(GN_OUT, CH_OUT, GRP, xt_hi, xt_lo)

            turn_rows(KT // 2, lambda: all_free(GN_WQ))
            pe.wait_ge(xt_lo_done, KT + KT)
            for k in range(2):
                full_group(GN_WQ + k, CH_WQ + k * CPG, xt_hi, xt_lo, 512, (GN_WQ + k) // 2)
            all_free(GN_U)
            for n in range(4):
                for r in range(2):
                    for h in range(NT):
                        mm = pe.transpose(side[:, n, r * S + h * P:r * S + (h + 1) * P],
                                          peer_q[:, h, (2 * n + r) * HD:(2 * n + r + 1) * HD], ident[:])
                mm.then_inc(pq_turned, 1)
            pe.wait_ge(subkeys_loaded, 16)
            pe.wait_ge(pq_copied, 4)
            for h in range(NT):
                for r in range(PH):
                    mm = pe.matmul(side[:, 2 * h + r // 4, (r % 4) * P:(r % 4 + 1) * P],
                                   peer_qt[:, r, tile_rows(h)], subkeys[:, r, :], start=True, stop=True)
                mm.then_inc(key_scores, 1)
            groups(GN_U, CH_U, GRP, xt_hi, xt_lo)

            pe.wait_ge(picks_ready, 1)
            for h in range(NT):
                for c in range(3):
                    mm = pe.transpose(side[:, h, c * P:(c + 1) * P],
                                      picks[:, h, c, :, :].rearrange("p a b -> p (a b)"), ident[:])
            mm.then_inc(picks_turned, 1)
            pe.wait_ge(picks_copied, 1)
            all_free(GN_V)
            for q in range(KT // 2):
                if q >= 4:
                    pe.wait_ge(act_copied, q - 3)
                for j in range(2):
                    for h in range(NT):
                        mm = pe.transpose(side[:, q % 4, j * S + h * P:j * S + (h + 1) * P],
                                          act_rows[:, h, (2 * q + j) * P:(2 * q + j + 1) * P], ident[:])
                mm.then_inc(act_turned, 1)
            for n in range(S // 16):
                pe.wait_ge(hot_ready, n + 1)
                if n >= 2:
                    pe.wait_ge(wmat_ready, n - 1)
                elif n == 0:
                    pe.wait_ge(act_copied, KT // 2)
                for t in range(16):
                    for g in range(3):
                        mm = pe.matmul(side[:, n % 2, t * 32:(t + 1) * 32], hot_c[:, t, :],
                                       hot_g[:, g, (n % 2) * 16 + t, :], start=(g == 0), stop=(g == 2))
                mm.then_inc(scattered, 1)
            pe.wait_ge(wmat_lo, S // 16)
            groups(GN_V, CH_V, GRP, xt_hi, xt_lo)

        @block.scalar
        def _(act):
            then = chain(act, act_chain)
            act.dma_start(g_mix[:], io["g_mix"]).then_inc(xt_loaded, 16)
            act.dma_start(xt_raw[:], io["xt"]).then_inc(xt_loaded, 16)
            act.dma_start(ident[:], io["ident"]).then_inc(const_loaded, 16)
            act.dma_start(g_ffn[:], io["g_ffn"]).then_inc(const_loaded, 16)
            act.dma_start(iotas[:], io["iotas"]).then_inc(const_loaded, 16)
            for name, t in (("causal", causal), ("dil", dil), ("strict", strict), ("rope", rope), ("tri", tri),
                            ("cmp_mask", cmp_mask), ("pe_t", pe_t), ("cmp_w2", cmp_w2)):
                act.dma_start(t[:], io[name]).then_inc(attn_loaded, 16)

            def hi(chunk, slot, width, m4):
                act.wait_ge(raw_loaded[slot], m4 * 16 + 16)
                if not (isinstance(chunk, int) and chunk < RING):
                    act.wait_ge(chunk_used, chunk - (RING - 1))
                nc.scalar.activation(w_hi[:, slot, 0:width], w_raw[:, slot, 0:width], ACT.Copy).then_inc(hi_ready, 1)

            def his(base_chunk, c0, c1, width, m4):
                for c in range(c0, c1):
                    hi(base_chunk + c, c % RING, width, m4 + c // RING)

            def evacuate_in(g, parity):
                act.wait_ge(chunk_used, g * CPG + CPG)
                for h in range(NT):
                    e = nc.scalar.activation(proj[:, h, bass.ds(g * W1C, W1C)], acc[:, parity, h, 0:W1C],
                                             ACT.Copy, scale=rstd_x[:, h:h + 1])
                e.then_inc(bank_free[parity], 1)

            act.wait_ge(xt_loaded, 32)
            for k in range(KT):
                nc.scalar.activation(xt_hi[:, k, :], xt_raw[:, k, :], ACT.Copy, scale=g_mix[:, k:k + 1])\
                    .then_inc(xt_hi_done, 1)
                if k % 2 and k // 2 < RING:
                    hi(k // 2, k // 2, 2 * W1C, 0)
            his(0, RING, CPG, 2 * W1C, 0)
            act.wait_ge(xt_lo_done, KT)
            act.dma_start(rows[:], io["x"]).then_inc(rows_loaded, 16)
            his(CPG, 0, 4, 2 * W1C, CPG // RING)
            act.wait_ge(rows_loaded, 16)
            for h in range(NT):
                e = nc.scalar.activation(rows[:, h, :], rows[:, h, :], ACT.Square, accum_out=ms_x[:, h:h + 1])
            e.then_inc(squares_done, 1)
            his(CPG, 4, 8, 2 * W1C, CPG // RING)
            act.wait_ge(rstd_ready, 1)
            evacuate_in(0, 0)
            his(CPG, 8, CPG, 2 * W1C, CPG // RING)
            with act.Fori(1, 5) as i:
                for g in range(2):
                    his(i * (2 * CPG) + g * CPG, 0, 4, 2 * W1C, i * (2 * CPG // RING) + g * CPG // RING)
                    evacuate_in(i * 2 + (g - 1), (g - 1) % 2)
                    his(i * (2 * CPG) + g * CPG, 4, CPG, 2 * W1C, i * (2 * CPG // RING) + g * CPG // RING)
            his(10 * CPG, 0, 4, 2 * W1C, 10 * CPG // RING)
            evacuate_in(9, 1)
            his(10 * CPG, 4, CPG, 2 * W1C, 10 * CPG // RING)
            evacuate_in(10, 0)

            act.wait_ge(bank_free[0], 6)
            act.wait_ge(bank_free[1], 5)
            nc.scalar.activation(nsa_gate.rearrange("p (a b) -> p a b", b=12), proj[:, :, C_CG:C_CG + 12],
                                 ACT.Sigmoid).then_inc(nsa_gate_ready, 1)
            for n in range(18):
                act.wait_ge(turned, n + 1)
                if n < 15:
                    w = 2 * S if n < 14 else S
                    src = side[:, n % 4, 0:w]
                    dst = feat[:, 2 * n:min(2 * n + 2, NTB), :].rearrange("p a b -> p (a b)")
                else:
                    b = 2 * (n - 15)
                    w = 2 * S if n < 17 else S
                    src = side[0:64, n % 4, 0:w]
                    dst = idx_t[:, b:min(b + 2, 5), :].rearrange("p a b -> p (a b)")
                nc.scalar.activation(dst, src, ACT.Copy).then_inc(turned_copied, 1)
            act.wait_ge(z_turned, 1)
            nc.scalar.activation(zt_hi[:].rearrange("p a b -> p (a b)"), side[:, 2, :], ACT.Copy).then_inc(z_hi_done, 1)
            act.wait_ge(attn_loaded, 128)
            for w in range(2):
                act.wait_ge(cmp_hidden, w + 1)
                nc.scalar.activation(cmp_h[:, w, :], side[:, 2, w * 32:w * 32 + NCMP], ACT.Gelu_apprx_tanh)\
                    .then_inc(cmp_act, 1)
                if w == 0:
                    act.dma_start(cmp_w1[:], io["cmp_w1"][1]).then_inc(cmp_loaded2, 16)

            def out_hi(n, src, dst, ready, need, done):
                act.wait_ge(ready, need)
                nc.scalar.activation(dst, src, ACT.Copy).then_inc(done, 1)

            n_out = 0
            for i, (br, h, part) in enumerate(passes):
                rows_n = 6 if br == "d" else 4
                nk = NCMP if (br, part) == ("c", 0) else S
                act.wait_ge(row_max_ready, i + 1)
                for r in range(rows_n):
                    m = r // 3 if br == "d" else r
                    e = nc.scalar.activation(probs[:, r, 0:nk], probs[:, r, 0:nk], ACT.Exp,
                                             bias=row_neg[:, m:m + 1], accum_out=row_den[:, r:r + 1])
                e.then_inc(exp_ready, 1)
                act.wait_ge(probs_turned, i + 1)
                if i:
                    act.wait_ge(pv_done, i)
                heads = 2 if br == "d" else 4
                if nk == NCMP:
                    nc.scalar.activation(probs_t[0:NCMP, 0, :, :].rearrange("p a b -> p (a b)"),
                                         side[0:NCMP, 0, :], ACT.Copy).then_inc(probs_copied, 1)
                else:
                    for s in range(2):
                        e = nc.scalar.activation(
                            probs_t[:, s, 0:heads, :].rearrange("p a b -> p (a b)"), side[:, s, 0:heads * P], ACT.Copy)
                    e.then_inc(probs_copied, 1)
                if last_of_output(br, part):
                    act.wait_ge(pv_done, i + 1)
                    nc.scalar.activation(ot_hi[:, ot_block[br]:ot_block[br] + heads, tile_rows(h)],
                                         side[:, 3, 0:heads * P].rearrange("p (a b) -> p a b", b=P),
                                         ACT.Copy).then_inc(out_hi_done, 1)
                    n_out += 1

            flat = lambda t: t[:].rearrange("p a b c -> p (a b c)")
            for u in range(2):
                act.wait_ge(stick_scores, u + 1)
                if u:
                    act.wait_ge(stick_out, u)
                then(nc.scalar.activation(flat(stick_z), side[:, 0:2, :].rearrange("p a b -> p (a b)"), ACT.Copy,
                                          scale=SCALE))
                then(nc.scalar.activation(flat(stick_l), flat(stick_z), ACT.Abs))
                then(nc.scalar.activation(flat(stick_l), flat(stick_l), ACT.Exp, scale=-1.0))
                nc.scalar.activation(flat(stick_l), flat(stick_l), ACT.Ln, bias=1.0).then_inc(stick_soft, 1)
                act.wait_ge(stick_arg, u + 1)
                nc.scalar.activation(flat(stick_e), flat(stick_e), ACT.Exp).then_inc(stick_exp, 1)
                act.wait_ge(stick_out, u + 1)
                nc.scalar.activation(ot_hi[:, 8 + 2 * u:10 + 2 * u, :].rearrange("p a b -> p (a b)"), side[:, 0, :],
                                     ACT.Copy).then_inc(stick_hi, 1)

            for i, (b0, n) in enumerate(BRANCHES):
                per = 1 + n // 2
                with act.Fori(0, GRP // 4) as m:
                    for k in range(4):
                        for j in range(per):
                            c = mix_chunk[i] + k * per + j
                            hi(m * (4 * per) + c, c % RING, 1024, m * per + c // RING)
                        j8 = i * GRP + k
                        act.wait_ge(chunk_used, m * (4 * per) + (mix_chunk[i] + k * per + 1))
                        if j8 >= 2:
                            act.wait_ge(gate_used, m * 4 + (j8 - 1))
                        for h in range(NT):
                            e = nc.scalar.activation(gate[:, k % 2, h, :], acc[:, 1, h, :], ACT.Sigmoid)
                        e.then_inc(bank_free[1], 1)

            def xt_hi_part(count0, gain):
                for q in range(KT // 2):
                    act.wait_ge(xt_turned, count0 + q + 1)
                    if gain is None:
                        nc.scalar.activation(xt_hi[:, 2 * q:2 * q + 2, :].rearrange("p a b -> p (a b)"),
                                             side[:, q % 4, :], ACT.Copy).then_inc(xt_hi_done, 1)
                    else:
                        for j in range(2):
                            e = nc.scalar.activation(xt_hi[:, 2 * q + j, :], side[:, q % 4, j * S:(j + 1) * S],
                                                     ACT.Copy, scale=gain[:, 2 * q + j:2 * q + j + 1])
                        e.then_inc(xt_hi_done, 1)

            def stream(ch0, n):
                with act.Fori(0, n) as m:
                    his(m * CPG + ch0, 0, CPG, 1024, m * (CPG // RING) + ch0 // RING)

            xt_hi_part(0, None)
            act.wait_ge(xt_turned, KT // 2)
            act.dma_start(rows[:], io["x"]).then_inc(rows_loaded, 16)
            act.wait_ge(gate_used, 4 * GRP)
            act.dma_start(subkeys[:], io["subkeys"]).then_inc(subkeys_loaded, 16)
            stream(CH_OUT, GRP)
            act.wait_ge(bank_free[GN_WQ % 2], GN_WQ // 2)
            act.wait_ge(bank_free[(GN_WQ + 1) % 2], (GN_WQ + 1) // 2)
            act.wait_ge(const_loaded, 48)
            xt_hi_part(KT // 2, g_ffn)
            his(CH_WQ, 0, 4, 1024, CH_WQ // RING)
            then(nc.scalar.activation(square[:], rows[:, 0, :], ACT.Square, accum_out=ms_h[:, 0:1]))
            nc.scalar.activation(square[:], rows[:, 1, :], ACT.Square, accum_out=ms_h[:, 1:2]).then_inc(squares_done, 1)
            his(CH_WQ, 4, 2 * CPG, 1024, CH_WQ // RING)
            act.wait_ge(rstd_ready, 2)
            for k in range(2):
                gn = GN_WQ + k
                act.wait_ge(chunk_used, CH_WQ + (k + 1) * CPG)
                for h in range(NT):
                    e = nc.scalar.activation(peer_q[:, h, k * 512:(k + 1) * 512], acc[:, gn % 2, h, :], ACT.Copy,
                                             scale=rstd_h[:, h:h + 1])
                e.then_inc(bank_free[gn % 2], 1)
            for n in range(4):
                act.wait_ge(pq_turned, n + 1)
                nc.scalar.activation(peer_qt[:, 2 * n:2 * n + 2, :].rearrange("p a b -> p (a b)"), side[:, n, :],
                                     ACT.Copy).then_inc(pq_copied, 1)
            for h in range(NT):
                act.wait_ge(key_scores, h + 1)
                e = nc.scalar.activation(key_s[:, h].rearrange("p a b c -> p (a b c)"),
                                         side[:, 2 * h:2 * h + 2, :].rearrange("p a b -> p (a b)"), ACT.Copy)
                e.then_inc(key_copied, 1)

            def evacuate_u(g, parity):
                act.wait_ge(chunk_used, g * CPG + (CH_U + CPG))
                for h in range(NT):
                    e = nc.scalar.activation(act_rows[:, h, bass.ds(g * 512, 512)], acc[:, parity, h, :],
                                             ACT.Gelu_apprx_tanh, scale=rstd_h[:, h:h + 1])
                e.then_inc(bank_free[parity], 1)

            m4 = CH_U // RING
            his(CH_U, 0, CPG, 1024, m4)
            his(CH_U + CPG, 0, 4, 1024, m4 + CPG // RING)
            evacuate_u(0, GN_U % 2)
            his(CH_U + CPG, 4, CPG, 1024, m4 + CPG // RING)
            with act.Fori(1, GRP // 2) as m:
                for k in range(2):
                    ch, in_slot = m * (2 * CPG) + (CH_U + k * CPG), m * (2 * CPG // RING) + (m4 + k * CPG // RING)
                    his(ch, 0, 4, 1024, in_slot)
                    evacuate_u(m * 2 + (k - 1), (GN_U + k - 1) % 2)
                    his(ch, 4, CPG, 1024, in_slot)
            evacuate_u(GRP - 1, (GN_U + GRP - 1) % 2)

            act.wait_ge(picks_shifted, 1)
            nc.scalar.activation(pair_v[:].rearrange("p a b c -> p (a b c)"),
                                 pair_v[:].rearrange("p a b c -> p (a b c)"), ACT.Exp).then_inc(picks_exp, 1)
            for q in range(KT // 2):
                act.wait_ge(act_turned, q + 1)
                nc.scalar.activation(act_t[:, 2 * q:2 * q + 2, :].rearrange("p a b -> p (a b)"), side[:, q % 4, :],
                                     ACT.Copy).then_inc(act_copied, 1)
            for n in range(S // 16):
                act.wait_ge(wmat_ready, n + 1)
                nc.scalar.activation(xt_hi[:, :, n * 16:(n + 1) * 16], wmat[:], ACT.Copy).then_inc(wmat_hi, 1)
            stream(CH_V, GRP)

        @block.vector
        def _(dve):
            then = chain(dve, dve_chain)

            def lo(chunk, slot, width):
                dve.wait_ge(hi_ready, chunk + 1)
                nc.vector.tensor_tensor(w_lo[:, slot, 0:width], w_raw[:, slot, 0:width],
                                        w_hi[:, slot, 0:width].bitcast(F32), ALU.subtract).then_inc(lo_ready, 1)

            def los(base_chunk, c0, c1, width=1024):
                for c in range(c0, c1):
                    lo(base_chunk + c, c % RING, width)

            dve.wait_ge(xt_loaded, 32)
            nc.vector.memset(half_exp, -0.5).then_inc(head_ms_done, 1)
            for k in range(KT):
                dve.wait_ge(xt_hi_done, k + 1)
                nc.vector.scalar_tensor_tensor(out=xt_lo[:, k, :], in0=xt_raw[:, k, :], scalar=g_mix[:, k:k + 1],
                                               in1=xt_hi[:, k, :].bitcast(F32), op0=ALU.mult, op1=ALU.subtract)\
                    .then_inc(xt_lo_done, 1)
                if k % 2 and k // 2 < RING:
                    lo(k // 2, k // 2, 2 * W1C)
            los(0, RING, CPG, 2 * W1C)
            with dve.Fori(1, NG1) as g:
                los(g * CPG, 0, CPG, 2 * W1C)

            dve.wait_ge(attn_loaded, 128)
            dve.wait_ge(gains_loaded, 16)
            dve.wait_ge(bank_free[0], 6)
            dve.wait_ge(bank_free[1], 5)
            for h in range(NT):
                if h:
                    dve.wait_ge(heads_ready, h)
                heads = proj[:, h, 0:NORMED * HD].rearrange("p (a b) -> p a b", b=HD)
                roped = proj[:, h, 0:ROPED * HD].rearrange("p (a b) -> p a b", b=HD)
                tmp = rope_tmp[:, 0:NORMED * HD].rearrange("p (a b) -> p a b", b=HD)
                then(nc.vector.tensor_tensor(tmp, heads, heads, ALU.mult))
                nc.vector.tensor_reduce(head_ms[:, 0:NORMED], tmp, AX, ALU.add).then_inc(head_ms_done, 1)
                dve.wait_ge(head_rstd_done, h + 1)
                then(nc.vector.tensor_tensor(heads, heads,
                                             head_rstd[:, 0:NORMED].unsqueeze(2).broadcast_to([P, NORMED, HD]), ALU.mult))
                for n, (a, b, g) in enumerate(GAIN_SPANS):
                    e = nc.vector.tensor_tensor(heads[:, a:b, :], heads[:, a:b, :],
                                                gains[:, g, :].unsqueeze(1).broadcast_to([P, b - a, HD]), ALU.mult)
                then(e)
                tmp = rope_tmp[:].rearrange("p (a b) -> p a b", b=HD)
                cosb = rope[:, 0, h, :].unsqueeze(1).broadcast_to([P, 2 * ROPED, 64])
                sinb = rope[:, 1, h, :].unsqueeze(1).broadcast_to([P, ROPED, 64])
                nsinb = rope[:, 2, h, :].unsqueeze(1).broadcast_to([P, ROPED, 64])
                nc.vector.tensor_tensor(tmp[:, :, 0:64], roped[:, :, 64:128], nsinb, ALU.mult)
                then(nc.vector.tensor_tensor(tmp[:, :, 64:128], roped[:, :, 0:64], sinb, ALU.mult))
                both = proj[:, h, 0:ROPED * HD].rearrange("p (a b) -> p a b", b=64)
                then(nc.vector.tensor_tensor(both, both, cosb, ALU.mult))
                e = nc.vector.tensor_tensor(roped, roped, tmp, ALU.add)
                e.then_inc(heads_ready, 1)
            dve.wait_ge(z_hi_done, 1)
            nc.vector.tensor_tensor(zt_lo[:].rearrange("p a b -> p (a b)"), side[:, 2, :],
                                    zt_hi[:].rearrange("p a b -> p (a b)").bitcast(F32), ALU.subtract)\
                .then_inc(z_lo_done, 1)

            for h in range(NT):
                dve.wait_ge(index_ready, h + 1)
                for i in range(4):
                    src = side[:, i // 2, (i % 2) * S:(i % 2 + 1) * S]
                    dst = idx_sum if i == 0 else idx_tmp
                    then(nc.vector.tensor_scalar(dst[:], src, 0.0, proj[:, h, C_IW + i:C_IW + i + 1],
                                                 ALU.max, ALU.mult))
                    if i:
                        then(nc.vector.tensor_tensor(idx_sum[:], idx_sum[:], idx_tmp[:], ALU.add))
                dve.nop().then_inc(index_read, 1)
                then(nc.vector.tensor_tensor(idx_sum[:], idx_sum[:], causal[:, h, :], ALU.add))
                for _r in range(S // 4 // 8):
                    then(nc.vector.max(top8, idx_sum[:]))
                    then(nc.vector.match_replace(idx_sum[:], top8, idx_sum[:], TAKEN))
                then(nc.vector.tensor_scalar(idx_tmp[:], idx_sum[:], -2e38, NEG, ALU.is_gt, ALU.mult))
                then(nc.vector.tensor_tensor(sel_mask[:, h, :], idx_tmp[:], causal[:, h, :], ALU.min))

            for w in range(2):
                src = feat[:, H_CKC + w, :].rearrange("p (n l) -> p l n", l=16)
                if w:
                    dve.wait_ge(cmp_hidden, 1)
                for a in range(2):
                    e = nc.vector.tensor_tensor(
                        cmp_b[:, a * 16:(a + 1) * 16, :], src[:, :, a:a + NCMP],
                        pe_t[:, w, a * 16:(a + 1) * 16].unsqueeze(2).broadcast_to([P, 16, NCMP]), ALU.add)
                e.then_inc(cmp_blocks, 1)
            dve.wait_ge(cmp_out, 1)
            then(nc.vector.tensor_copy(k_cmp[:], cmp_outs[0]))
            then(nc.vector.tensor_tensor(k_sq[:], k_cmp[:], k_cmp[:], ALU.mult))
            nc.vector.tensor_reduce(k_ms, k_sq[:], AX, ALU.add).then_inc(cmp_square, 1)
            dve.wait_ge(cmp_rstd, 1)
            dve.wait_ge(cmp_out, 2)
            nc.vector.scalar_tensor_tensor(out=k_cmp[:], in0=k_cmp[:], scalar=k_rstd, in1=gains_cmp[:],
                                           op0=ALU.mult, op1=ALU.mult).then_inc(cmp_normed, 1)
            nc.vector.tensor_copy(v_cmp[:], cmp_outs[1])
            dve.wait_ge(cmp_turned, 1)
            nc.vector.tensor_copy(kt_cmp[:], side[:, 2, 64:64 + NCMP]).then_inc(cmp_ready, 1)

            dve.wait_ge(nsa_gate_ready, 1)
            n_out = 0
            for i, (br, h, part) in enumerate(passes):
                nk = NCMP if (br, part) == ("c", 0) else S
                rows_n = 6 if br == "d" else 4
                heads = 2 if br == "d" else 4
                p = probs[:, 0:rows_n, 0:nk]
                dve.wait_ge(scores_ready, i + 1)
                if br == "d":
                    for s in range(2):
                        src = side[:, 0:3, :].rearrange("p a (b c) -> p (a b) c", c=S)[:, 3 * s:3 * s + 3, :]
                        e = nc.vector.scalar_tensor_tensor(
                            out=probs[:, 3 * s:3 * s + 3, :].rearrange("p a b -> p (a b)"),
                            in0=src.rearrange("p a b -> p (a b)"), scalar=SCALE,
                            in1=dil[:, h].rearrange("p a b -> p (a b)"), op0=ALU.mult, op1=ALU.add)
                    then(e)
                    then(nc.vector.tensor_reduce(row_max[:, 0:2], probs[:].rearrange("p (s g) k -> p s (g k)", g=3),
                                                 AX, ALU.max))
                else:
                    src = side[:, 0:2, :].rearrange("p a (b c) -> p (a b) c", c=S)[:, :, 0:nk]
                    mask = sel_mask[:, h, :] if br == "b" else cmp_mask[:, h, :] if part == 0 else causal[:, h, :]
                    then(nc.vector.scalar_tensor_tensor(
                        out=p, in0=src, scalar=SCALE, in1=mask.unsqueeze(1).broadcast_to([P, 4, nk]),
                        op0=ALU.mult, op1=ALU.add))
                    then(nc.vector.tensor_reduce(row_max[:, 0:4], p, AX, ALU.max))
                nc.vector.tensor_scalar(row_neg[:, 0:heads], row_max[:, 0:heads], -1e37, -1.0, ALU.max, ALU.mult)\
                    .then_inc(row_max_ready, 1)
                dve.wait_ge(exp_ready, i + 1)
                if br == "d":
                    then(nc.vector.tensor_reduce(row_den[:, 0:2], row_den[:, 0:6].rearrange("p (s g) -> p s g", g=3),
                                                 AX, ALU.add))
                then(nc.vector.tensor_scalar(row_den[:, 0:heads], row_den[:, 0:heads], TINY, None, ALU.max))
                then(nc.vector.reciprocal(row_inv[:, 0:heads], row_den[:, 0:heads]))
                if br == "c":
                    g = nsa_gate[:, h * 12:(h + 1) * 12].rearrange("p (a b) -> p a b", b=3)[:, :, part]
                    then(nc.vector.tensor_tensor(row_inv[:, 0:4], row_inv[:, 0:4], g, ALU.mult))
                if br == "d":
                    sg = probs[:].rearrange("p (s g) k -> p s g k", g=3)
                    then(nc.vector.tensor_tensor(sg[:, :, 0, :], sg[:, :, 0, :], sg[:, :, 1, :], ALU.add))
                    then(nc.vector.tensor_tensor(sg[:, :, 0, :], sg[:, :, 0, :], sg[:, :, 2, :], ALU.add))
                    q = sg[:, :, 0, :]
                else:
                    q = p
                nc.vector.tensor_tensor(q, q, row_inv[:, 0:heads].unsqueeze(2).broadcast_to([P, heads, nk]), ALU.mult)\
                    .then_inc(probs_ready, 1)
                if last_of_output(br, part):
                    n_out += 1
                    dve.wait_ge(out_hi_done, n_out)
                    nc.vector.tensor_tensor(
                        ot_lo[:, ot_block[br]:ot_block[br] + heads, tile_rows(h)],
                        side[:, 3, 0:heads * P].rearrange("p (a b) -> p a b", b=P),
                        ot_hi[:, ot_block[br]:ot_block[br] + heads, tile_rows(h)].bitcast(F32),
                        ALU.subtract).then_inc(out_lo_done, 1)
                dve.wait_ge(probs_turned, i + 1)

            z2 = stick_z[:].rearrange("p r s t -> p r (s t)")
            e2 = stick_e[:].rearrange("p r s t -> p r (s t)")
            l2 = stick_l[:].rearrange("p r s t -> p r (s t)")
            smask = strict[:].rearrange("p s t -> p (s t)").unsqueeze(1).broadcast_to([P, 2, 2 * S])
            for u in range(2):
                dve.wait_ge(stick_soft, u + 1)
                then(nc.vector.scalar_tensor_tensor(out=l2, in0=z2, scalar=0.0, in1=l2, op0=ALU.max, op1=ALU.add))
                nc.vector.tensor_tensor(l2, l2, smask, ALU.mult).then_inc(stick_masked, 1)
                dve.wait_ge(stick_sums, u + 1)
                then(nc.vector.tensor_tensor(e2, z2, side[:, 2:4, :], ALU.add))
                nc.vector.tensor_scalar(e2, e2, 0.0, None, ALU.min).then_inc(stick_arg, 1)
                dve.wait_ge(stick_exp, u + 1)
                nc.vector.tensor_tensor(e2, e2, smask, ALU.mult).then_inc(stick_weights, 1)
                dve.wait_ge(stick_hi, u + 1)
                nc.vector.tensor_tensor(ot_lo[:, 8 + 2 * u:10 + 2 * u, :].rearrange("p a b -> p (a b)"), side[:, 0, :],
                                        ot_hi[:, 8 + 2 * u:10 + 2 * u, :].rearrange("p a b -> p (a b)").bitcast(F32),
                                        ALU.subtract).then_inc(stick_lo, 1)

            def mix_los(i, m, k):
                per = 1 + BRANCHES[i][1] // 2
                for j in range(per):
                    c = mix_chunk[i] + k * per + j
                    lo(m * (4 * per) + c, c % RING, 1024)

            def merge(i, m, k):
                per = 1 + BRANCHES[i][1] // 2
                j8 = i * GRP + k
                dve.wait_ge(bank_free[1], m * 4 + (GN_MIX // 2 + j8 + 1))
                dve.wait_ge(chunk_used, m * (4 * per) + (mix_chunk[i] + (k + 1) * per))
                freed = m * 4 + ((GN_MIX + 1) // 2 + j8 + 1)
                for h in range(NT):
                    dst = rows[:, h, bass.ds(m * 2048 + k * 512, 512)] if i == 0 else gate[:, k % 2, h, :]
                    e = nc.vector.tensor_tensor(dst, acc[:, 0, h, :], gate[:, k % 2, h, :], ALU.mult)
                e.then_inc(bank_free[0], 1)
                dve.wait_ge(bank_free[0], freed)
                if i == 0:
                    dve.nop().then_inc(gate_used, 1)
                else:
                    for h in range(NT):
                        dst = rows[:, h, bass.ds(m * 2048 + k * 512, 512)]
                        e = nc.vector.tensor_tensor(dst, dst, gate[:, k % 2, h, :], ALU.add)
                    e.then_inc(gate_used, 1)

            mix_los(0, 0, 0)
            for i in range(4):
                with dve.Fori(0, GRP // 4 - 1) as m:
                    for k in range(4):
                        mix_los(i, m, k + 1)
                        merge(i, m, k)
                for k in range(4):
                    if k < 3:
                        mix_los(i, GRP // 4 - 1, k + 1)
                    elif i < 3:
                        mix_los(i + 1, 0, 0)
                    merge(i, GRP // 4 - 1, k)

            def xt_lo_part(count0, gain):
                for q in range(KT // 2):
                    dve.wait_ge(xt_hi_done, KT + count0 + q + 1)
                    if gain is None:
                        e = nc.vector.tensor_tensor(
                            xt_lo[:, 2 * q:2 * q + 2, :].rearrange("p a b -> p (a b)"), side[:, q % 4, :],
                            xt_hi[:, 2 * q:2 * q + 2, :].rearrange("p a b -> p (a b)").bitcast(F32), ALU.subtract)
                    else:
                        for j in range(2):
                            e = nc.vector.scalar_tensor_tensor(
                                out=xt_lo[:, 2 * q + j, :], in0=side[:, q % 4, j * S:(j + 1) * S],
                                scalar=gain[:, 2 * q + j:2 * q + j + 1],
                                in1=xt_hi[:, 2 * q + j, :].bitcast(F32), op0=ALU.mult, op1=ALU.subtract)
                    e.then_inc(xt_lo_done, 1)

            def add_rows(g, ch0, parity):
                dve.wait_ge(chunk_used, g * CPG + (ch0 + CPG))
                for h in range(NT):
                    dst = rows[:, h, bass.ds(g * 512, 512)]
                    e = nc.vector.tensor_tensor(dst, acc[:, parity, h, :], dst, ALU.add)
                e.then_inc(bank_free[parity], 1)

            def residual_groups(gn0, ch0):
                los(ch0, 0, CPG)
                los(ch0 + CPG, 0, 4)
                add_rows(0, ch0, gn0 % 2)
                los(ch0 + CPG, 4, CPG)
                with dve.Fori(1, GRP // 2) as m:
                    for k in range(2):
                        los(m * (2 * CPG) + (ch0 + k * CPG), 0, 4)
                        add_rows(m * 2 + (k - 1), ch0, (gn0 + k - 1) % 2)
                        los(m * (2 * CPG) + (ch0 + k * CPG), 4, CPG)
                add_rows(GRP - 1, ch0, (gn0 + GRP - 1) % 2)

            xt_lo_part(0, None)
            dve.wait_ge(rows_loaded, 32)
            residual_groups(GN_OUT, CH_OUT)
            xt_lo_part(KT // 2, g_ffn)
            los(CH_WQ, 0, 2 * CPG)

            dve.wait_ge(key_copied, NT)

            def rank_keys(r, h, side_i):
                src = key_s[:, h, r, side_i, :]
                v, n = key_v[:, h, r, side_i, :], key_i[:, h, r, side_i, :]
                then(nc.vector.max(v[:, 0:8], src))
                nc.vector.max_index(n[:, 0:8], v[:, 0:8], src)
                then(nc.vector.match_replace(key_w[:], v[:, 0:8], src, TAKEN))
                then(nc.vector.max(v[:, 8:16], key_w[:]))
                then(nc.vector.max_index(n[:, 8:16], v[:, 8:16], key_w[:]))

            def pair_grid(r, h):
                v = key_v[:, h, r]
                then(nc.vector.tensor_tensor(cand[:], v[:, 0, :].unsqueeze(2).broadcast_to([P, PK, PK]),
                                             v[:, 1, :].unsqueeze(1).broadcast_to([P, PK, PK]), ALU.add))

            def rank_pairs(r, h, second):
                c = cand[:].rearrange("p a b -> p (a b)")
                v, n = pair_v[:, h, r, 8 * second:8 * second + 8], pair_i[:, h, r, 8 * second:8 * second + 8]
                then(nc.vector.max(v, c))
                then(nc.vector.max_index(n, v, c))
                if not second:
                    then(nc.vector.match_replace(c, v, c, TAKEN))

            def place_pairs(r, h):
                n = pair_i[:, h, r, :]
                nc.vector.tensor_scalar(pair_n[:, 0, :], n, 4, None, ALU.logical_shift_right)
                then(nc.vector.tensor_scalar(pair_n[:, 1, :], n, 15, None, ALU.bitwise_and))
                nc.vector.tensor_copy(pair_f[:], pair_n[:])
                then(nc.vector.tensor_copy(key_f[:], key_i[:, h, r]))

            def look_up(r, h, side_i):
                then(nc.vector.tensor_tensor(cand[:], pair_f[:, side_i, :].unsqueeze(2).broadcast_to([P, PK, PK]),
                                             iotas[:, 0:PK].unsqueeze(1).broadcast_to([P, PK, PK]), ALU.is_equal))
                then(nc.vector.tensor_tensor(cand[:], cand[:],
                                             key_f[:, side_i, :].unsqueeze(1).broadcast_to([P, PK, PK]), ALU.mult))
                then(nc.vector.tensor_reduce(picks[:, h, side_i, r, :], cand[:], AX, ALU.add))

            def split_place(r, h):
                then(nc.vector.tensor_copy(pick_n[:, 0, :], picks[:, h, 1, r, :]))
                then(nc.vector.tensor_scalar(pick_n[:, 1, :], pick_n[:, 0, :], 1, 6, ALU.bitwise_and,
                                             ALU.logical_shift_left))
                then(nc.vector.tensor_scalar(pick_n[:, 0, :], pick_n[:, 0, :], 1, None, ALU.logical_shift_right))
                then(nc.vector.tensor_copy(pair_f[:], pick_n[:]))
                nc.vector.tensor_copy(picks[:, h, 1, r, :], pair_f[:, 0, :])
                then(nc.vector.tensor_tensor(picks[:, h, 0, r, :], picks[:, h, 0, r, :], pair_f[:, 1, :], ALU.add))

            for r in range(PH):
                ch = CH_U + r * CPG
                for h in range(NT):
                    c = h * 8
                    los(ch, c, c + 1)
                    rank_keys(r, h, 0)
                    los(ch, c + 1, c + 2)
                    rank_keys(r, h, 1)
                    los(ch, c + 2, c + 3)
                    pair_grid(r, h)
                    rank_pairs(r, h, 0)
                    los(ch, c + 3, c + 4)
                    rank_pairs(r, h, 1)
                    los(ch, c + 4, c + 5)
                    place_pairs(r, h)
                    los(ch, c + 5, c + 6)
                    look_up(r, h, 0)
                    los(ch, c + 6, c + 7)
                    look_up(r, h, 1)
                    los(ch, c + 7, c + 8)
                    split_place(r, h)
            pv = pair_v[:].rearrange("p h r k -> p (h r) k")
            then(nc.vector.tensor_copy(soft_inv, pv[:, :, 0]))
            nc.vector.tensor_tensor(pv, pv, soft_inv.unsqueeze(2).broadcast_to([P, NT * PH, PK]), ALU.subtract)\
                .then_inc(picks_shifted, 1)
            dve.wait_ge(picks_exp, 1)
            then(nc.vector.tensor_reduce(soft_den, pv, AX, ALU.add))
            then(nc.vector.reciprocal(soft_inv, soft_den))
            for h in range(NT):
                e = nc.vector.tensor_tensor(picks[:, h, 2], pair_v[:, h],
                                            soft_inv[:, h * PH:(h + 1) * PH].unsqueeze(2).broadcast_to([P, PH, PK]),
                                            ALU.mult)
            e.then_inc(picks_ready, 1)
            dve.wait_ge(picks_turned, 1)
            for h in range(NT):
                e = nc.vector.tensor_copy(kmaj[:, :, tile_rows(h)],
                                          side[:, h, 0:3 * P].rearrange("p (c t) -> p c t", t=P))
            e.then_inc(picks_copied, 1)
            dve.wait_ge(picks_copied, 1)
            g16 = hot_g[:].rearrange("p a b c -> p (a b c)")[:, 0:S]
            dve.wait_ge(act_turned, KT // 2)
            src = kmaj[:, 2, :]
            for part in range(3):
                then(nc.vector.tensor_copy(g16, src))
                then(nc.vector.tensor_copy(g_parts[:, 2 * part, :], g16))
                if part < 2:
                    then(nc.vector.tensor_tensor(g_parts[:, 2 * part + 1, :], src, g_parts[:, 2 * part, :],
                                                 ALU.subtract))
                    src = g_parts[:, 2 * part + 1, :]
            for n in range(S // 16 + 1):
                if n < S // 16:
                    t = slice(n * 16, (n + 1) * 16)
                    if n:
                        dve.wait_ge(scattered, n)
                    nc.vector.tensor_tensor(hot_c[:], kmaj[:, 0, t].unsqueeze(2).broadcast_to([P, 16, P]),
                                            iotas[:].unsqueeze(1).broadcast_to([P, 16, P]), ALU.is_equal)
                    then(nc.vector.tensor_tensor(hot_q[:, 0:16, :], kmaj[:, 1, t].unsqueeze(2).broadcast_to([P, 16, 32]),
                                                 iotas[:, 0:32].unsqueeze(1).broadcast_to([P, 16, 32]), ALU.is_equal))
                    for g in range(3):
                        e = nc.vector.tensor_tensor(hot_g[:, g, (n % 2) * 16:(n % 2) * 16 + 16, :], hot_q[:, 0:16, :],
                                                    g_parts[:, 2 * g, t].unsqueeze(2).broadcast_to([P, 16, 32]), ALU.mult)
                    e.then_inc(hot_ready, 1)
                if n:
                    m = n - 1
                    t = slice(m * 16, (m + 1) * 16)
                    dve.wait_ge(scattered, m + 1)
                    if m:
                        dve.wait_ge(wmat_lo, m)
                    nc.vector.tensor_tensor(wmat[:], side[:, m % 2, :].rearrange("p (t q) -> p q t", q=32),
                                            act_t[:, :, t], ALU.mult).then_inc(wmat_ready, 1)
                    dve.wait_ge(wmat_hi, m + 1)
                    nc.vector.tensor_tensor(xt_lo[:, :, t], wmat[:], xt_hi[:, :, t].bitcast(F32),
                                            ALU.subtract).then_inc(wmat_lo, 1)
            residual_groups(GN_V, CH_V)

        @block.gpsimd
        def _(pool):
            then = chain(pool, pool_chain)
            pool.dma_start(gains_cmp[:], io["gain_cmp"]).then_inc(gain_cmp_loaded, 16)

            def rsqrt_mean(out, total, n, parts=P):
                w = out.shape[1]
                then(nc.gpsimd.tensor_scalar(out, total, 1.0 / n, EPS, ALU.mult, ALU.add))
                return nc.gpsimd.tensor_tensor(out, out, half_exp[0:parts, 0:w], ALU.pow)

            pool.wait_ge(head_ms_done, 1)
            pool.wait_ge(squares_done, 1)
            rsqrt_mean(rstd_x, ms_x, D).then_inc(rstd_ready, 1)
            pool.dma_start(cmp_w1[:], io["cmp_w1"][0]).then_inc(cmp_loaded, 16)
            pool.dma_start(gains[:], io["gains"]).then_inc(gains_loaded, 16)
            for h in range(NT):
                pool.wait_ge(head_ms_done, h + 2)
                rsqrt_mean(head_rstd[:, 0:NORMED], head_ms[:, 0:NORMED], HD).then_inc(head_rstd_done, 1)
            pool.wait_ge(gain_cmp_loaded, 16)
            pool.wait_ge(cmp_square, 1)
            rsqrt_mean(k_rstd, k_ms, HD, NCMP).then_inc(cmp_rstd, 1)
            pool.wait_ge(squares_done, 2)
            rsqrt_mean(rstd_h, ms_h, D).then_inc(rstd_ready, 1)
            with pool.Fori(0, GRP // 2) as m:
                for k in range(2):
                    gn = GN_V + k
                    pool.wait_ge(bank_free[gn % 2], m + (gn // 2 + 1))
                    pool.dma_start(io["out"][:, :, bass.ds(m * 1024 + k * 512, 512)],
                                   rows[:, :, bass.ds(m * 1024 + k * 512, 512)]).then_inc(stored, 16)
            pool.wait_ge(stored, 16 * GRP)


def tiles(w, width):
    k, n = w.shape
    return (w.reshape(k // 256, 2, P, n // width, width).transpose(3, 0, 2, 1, 4)
            .reshape(n // width, k // 256, P, 2 * width))


def kernel(x, norm_mix, w_in, qk_gain, nsa_pe, nsa_w1, nsa_w2, gate_down, gate_up, w_branch, w_out,
           norm_ffn, peer_wq, peer_subkeys, peer_u, peer_v):
    import concourse.bacc as bacc
    from concourse.bass_utils import run_bass_kernel_spmd

    arr = {k: np.asarray(v) for k, v in dict(
        x=x, norm_mix=norm_mix, w_in=w_in, qk_gain=qk_gain, nsa_pe=nsa_pe, nsa_w1=nsa_w1, nsa_w2=nsa_w2,
        gate_down=gate_down, gate_up=gate_up, w_branch=w_branch, w_out=w_out, norm_ffn=norm_ffn,
        peer_wq=peer_wq, peer_subkeys=peer_subkeys, peer_u=peer_u, peer_v=peer_v).items()}
    f = np.float32
    widths = (512, 512, 512, 512, 128, 128, 256, 64, 4, 512, 128, 128, 128, 128, 128, 128, 12, 768, 256, 256)
    names = ("aq", "ak", "av", "bq", "bk", "bv", "biq", "bik", "biw", "cq", "ckc", "cvc", "cks", "cvs", "ckw", "cvw",
             "cg", "dq", "dk", "dv")
    col = dict(zip(names, np.split(arr["w_in"][0], np.cumsum(widths)[:-1], axis=1)))
    w1 = np.concatenate([col[n] for n in ("bq", "bk", "cq", "cks", "ckw", "dq", "dk", "ckc", "cvc", "biq", "bik", "biw",
                                          "bv", "cvs", "cvw", "dv", "cg", "aq", "ak", "av")]
                        + [arr["gate_down"][0]], axis=1)
    wb = np.split(arr["w_branch"][0], (512, 1024, 1536), axis=0)
    parts = []
    for b in (1, 2, 0, 3):
        gu, w = tiles(arr["gate_up"][0, b], 512), tiles(wb[b], 512)
        parts.append(np.concatenate([gu, w], axis=1).reshape(-1, P, 1024))
    parts.append(tiles(arr["w_out"][0], 512).reshape(-1, P, 1024))
    parts.append(tiles(arr["peer_wq"][0], 512).reshape(-1, P, 1024))
    order = lambda w: w.reshape(64, 32, 2, D).transpose(1, 2, 0, 3).reshape(D, D)
    parts.append(tiles(order(arr["peer_u"][0]).T, 512).reshape(-1, P, 1024))
    parts.append(tiles(order(arr["peer_v"][0]), 512).reshape(-1, P, 1024))
    stream = np.concatenate(parts, axis=0)
    sk = np.zeros((P, PH, P), f)
    for b in range(2):
        sk[64 * b:64 * b + 64, :, 64 * b:64 * b + 64] = arr["peer_subkeys"][0, :, b].transpose(2, 0, 1)

    t = np.arange(S)
    d = t[:, None] - t[None, :]
    by_tile = lambda m: np.ascontiguousarray(m.reshape((NT, P) + m.shape[1:]).swapaxes(0, 1), dtype=f)
    keep = lambda m: np.where(m, 0.0, NEG).astype(f)
    dil = np.stack([keep((d >= 0) & (d <= w) & (d % r == 0)) for w, r in ((128, 1), (512, 4), (2048, 16))], axis=1)
    inv = f(10000.0) ** (-np.arange(0, HD, 2, dtype=f) / f(HD))
    ang = (t.astype(f)[:, None] * inv[None, :]).astype(f)
    rope = np.stack([by_tile(np.cos(ang)), by_tile(np.sin(ang)), by_tile(-np.sin(ang))], axis=1)
    k = np.arange(P)
    host = {
        "w_in": tiles(w1, W1C).reshape(-1, P, 2 * W1C),
        "stream": stream,
        "xt": arr["x"][0].T.reshape(KT, P, S).transpose(1, 0, 2),
        "x": arr["x"][0].reshape(NT, P, D).transpose(1, 0, 2),
        "g_mix": arr["norm_mix"][0].reshape(KT, P).T,
        "g_ffn": arr["norm_ffn"][0].reshape(KT, P).T,
        "gains": arr["qk_gain"][0].reshape(1, 8, HD),
        "gain_cmp": arr["qk_gain"][0][3:4],
        "cmp_w1": arr["nsa_w1"][0].transpose(0, 2, 1, 3),
        "cmp_w2": arr["nsa_w2"][0].transpose(1, 0, 2),
        "pe_t": arr["nsa_pe"][0].transpose(2, 0, 1),
        "subkeys": sk,
        "ident": np.eye(P, dtype=f),
        "iotas": np.broadcast_to(np.arange(P, dtype=f), (P, P)),
        "causal": by_tile(keep(d >= 0)),
        "dil": by_tile(dil),
        "strict": by_tile((d > 0).T.astype(f)),
        "rope": rope,
        "tri": np.stack([-(k[:, None] >= k[None, :]).astype(f), -np.ones((P, P), f)], axis=1),
        "cmp_mask": by_tile(keep(t[:, None] >= 16 * np.arange(NCMP)[None, :] + 31)),
    }
    host = {n: np.ascontiguousarray(a) for n, a in host.items()}
    nc = bacc.Bacc("TRN2", target_bir_lowering=False, num_devices=1)
    io, maps = {}, {}
    for n, a in host.items():
        io[n] = nc.dram_tensor("in_" + n, a.shape, F32, kind="ExternalInput").ap()
        maps["in_" + n] = a
    out = nc.dram_tensor("out_h", (1, S, D), F32, kind="ExternalOutput").ap()
    io["out"] = out.rearrange("a (h p) d -> p (a h) d", p=P)
    io["gains"] = io["gains"].rearrange("a g d -> a (g d)").broadcast_to([P, 8 * HD]).rearrange("p (g d) -> p g d", d=HD)
    io["gain_cmp"] = io["gain_cmp"].broadcast_to([NCMP, HD])
    build(nc, io)
    r = run_bass_kernel_spmd(nc, [maps], core_ids=[0])
    return r.results[0]["out_h"]
```

```python
import numpy as np

import concourse.bass as bass
from concourse import mybir

F32 = mybir.dt.float32
F32R = mybir.dt.float32r
U32 = mybir.dt.uint32
ALU = mybir.AluOpType
ACT = mybir.ActivationFunctionType
AX = mybir.AxisListType.X

P = 128
S = 256
NT = S // P
D = 4096
KT = D // P
HD = 128
EPS = 1e-6
SCALE = HD ** -0.5
NEG = -1e38
TAKEN = -3e38
TINY = float(np.finfo(np.float32).tiny)

B_Q, B_K, B_KC, B_IQ, B_IK, B_IW, B_CG, B_VC, B_V = 0, 512, 640, 768, 1024, 1088, 1092, 1104, 1232
C_Q, C_VS, C_VW = 1360, 2128, 2256
D_Q, D_V = 2384, 3408
Z_COL = 3664
A_Q, A_V = 3920, 4944
NCOL = 5456
NG1 = 11
W1C = NCOL // NG1
assert NG1 * W1C == NCOL and W1C <= 512
HEADS = {
    "b": (B_Q, 6, 5, ((0, 4, 0), (4, 5, 1))),
    "c": (C_Q, 6, 6, ((0, 4, 2), (4, 5, 4), (5, 6, 5))),
    "d": (D_Q, 8, 8, ((0, 6, 6), (6, 8, 7))),
}
OUT_COL = {"b": B_Q, "c": C_Q, "d": D_Q, "a": A_Q}

RING = 4
LEAD = RING - 1
CPG = KT // 2
GRP = D // 512
MERGE = ("b", "c", "d", "a")
MIX_K = {"b": 4, "c": 4, "d": 2, "a": 4}
CH_MIX = NG1 * CPG
MIX_CH, _c = {}, CH_MIX
for _b in MERGE:
    MIX_CH[_b] = _c
    _c += GRP * (1 + MIX_K[_b] // 2)
CH_OUT = _c
CH_WQ = CH_OUT + GRP * CPG
CH_U = CH_WQ + 2 * CPG
CH_V = CH_U + GRP * CPG
CH_END = CH_V + GRP * CPG
GN_MIX = NG1
GN_OUT = GN_MIX + 2 * 4 * GRP
GN_WQ = GN_OUT + GRP
GN_U = GN_WQ + 2
GN_V = GN_U + GRP

NCMP = (S - 32) // 16 + 1
PH, PK = 8, 16
KB = 1024
NX2 = 24
HOT = 8
ROUNDS = S // HOT

B_READY, C_READY, D_READY, A_READY = 51, 83, 131, 179


NORM_AT = {"b": 52, "c": 85, "d": 132}
NORM_STEP = {"b": 1, "c": 2, "d": 2}
TURNS = [(52, 0, "i", (0, 1)), (53, 1, "i", (2, 3)), (54, 2, "i", (4,)),
         (61, 2, "b", (5, 6)), (62, 3, "b", (0, 1)), (64, 2, "b", (2, 3)), (65, 3, "b", (4,)),
         (98, 3, "c", (0, 1)), (100, 2, "c", (2, 3)), (101, 3, "c", (4, 5)),
         (144, 2, "d", (0, 1)), (146, 2, "d", (2, 3)), (148, 2, "d", (4, 5)), (150, 2, "d", (6, 7)),
         (182, 0, "a", (0, 1)), (183, 1, "a", (2, 3)), (184, 2, "a", (4, 5)), (185, 3, "a", (6, 7))]
Z_TURN = 152
INDEX_AT = (57, 64)
INDEX_READ = (61, 68)
CMP_HID = (73, 77, 81, 85)
CMP_LOAD = (60, 76, 80, 84)
CMP_OUT = 89
PASSES = [("b", 0, 0), ("b", 1, 0),
          ("c", 0, 1), ("c", 0, 2), ("c", 0, 0), ("c", 1, 1), ("c", 1, 2), ("c", 1, 0),
          ("d", 0, 0), ("d", 1, 0)]
PASS_AT = (75, 82, 104, 111, 118, 125, 132, 139, 157, 165)
STICK_AT = (189, 211)
SQUARES_X, SQUARES_H = 14, CH_WQ + 6
RANK_AT, RANK_STEP = CH_U - 2, 5
SHARED_LO = range(CH_U + 5, RANK_AT + 16 * RANK_STEP, 2)
SOFTMAX_AT = RANK_AT + 16 * RANK_STEP + 1
PICKS_TURN = SOFTMAX_AT + 3
SCATTER_AT = PICKS_TURN + LEAD + 1
assert SCATTER_AT + ROUNDS + LEAD < CH_V


def first_part(br, part):
    return br != "c" or part == 1


def last_part(br, part):
    return br != "c" or part == 0


def build(nc, io):
    base = (nc.sbuf_base + 31) // 32 * 32
    XT0 = base
    RG0 = XT0 + 64 * KB
    MG0 = RG0 + 12 * RING * KB
    CN0 = MG0 + 32 * KB

    def at(name, shape, dt, off):
        return nc.alloc_sbuf_tensor_at(name, shape, dt, offset=off)

    cursor = [CN0]

    def const(name, shape, dt=F32):
        t = at(name, shape, dt, cursor[0])
        cursor[0] += (int(np.prod(shape[1:])) * 4 + 31) // 32 * 32
        assert cursor[0] <= nc.sbuf_usable_end, name
        return t

    xt_hi = at("xt_hi", [P, KT, S], F32R, XT0)
    xt_lo = at("xt_lo", [P, KT, S], F32R, XT0 + 32 * KB)
    w_raw = at("w_raw", [P, RING, 1024], F32, RG0)
    w_hi = at("w_hi", [P, RING, 1024], F32R, RG0 + 4 * RING * KB)
    w_lo = at("w_lo", [P, RING, 1024], F32R, RG0 + 8 * RING * KB)
    xt_raw = at("xt_raw", [P, KT, S], F32, MG0)
    rows = at("rows", [P, NT, D], F32, MG0)
    cmp_w1 = at("cmp_w1", [P, 16, P], F32, MG0)
    feat = {"c": at("feat_c", [P, 6, S], F32, MG0), "b": at("feat_b", [P, 7, S], F32, MG0 + 8 * KB),
            "d": at("feat_d", [P, 8, S], F32, MG0 + 8 * KB), "a": at("feat_a", [P, 8, S], F32, XT0),
            "i": at("idx_t", [64, 5, S], F32, MG0 + 16 * KB)}
    probs = at("probs", [P, 6, S], F32, MG0 + 16 * KB)
    probs_t = at("probs_t", [P, 2, 4, P], F32, MG0 + 22 * KB)
    sel_mask = at("sel_mask", [P, NT, S], F32, MG0 + 26 * KB)
    idx_tmp = at("idx_tmp", [P, S], F32, MG0 + 28 * KB)
    idx_sum = at("idx_sum", [P, S], F32, MG0 + 29 * KB)
    rope_tmp = at("rope_tmp", [P, 8 * HD], F32, MG0 + 28 * KB)

    ident = const("ident", [P, P])
    g_mix = const("g_mix", [P, KT])
    g_ffn = const("g_ffn", [P, KT])
    small = const("small", [P, 320])
    PJ0 = cursor[0]
    proj = const("proj", [P, NT, NCOL])
    row = NCOL * 4

    def over(name, shape, col):
        return (at(name + "_hi", shape, F32R, PJ0 + col * 4), at(name + "_lo", shape, F32R, PJ0 + row + col * 4))

    ot = {b: over("ot_" + b, [P, NT, MIX_K[b], P], OUT_COL[b]) for b in MERGE}
    zt = over("zt", [P, NT, 2, P], D_Q + 512)
    tail0 = cursor[0]
    causal = const("causal", [P, NT, S])
    dil = const("dil", [P, NT, 3, S])
    gate = at("gate", [P, 2, NT, 512], F32, tail0)
    rope = const("rope", [P, 3, NT, 64])
    gains = const("gains", [P, 8, HD])
    cmp_mask = const("cmp_mask", [P, NT, NCMP])
    pe_t = const("pe_t", [P, 2, 32])
    cmp_w2 = const("cmp_w2", [P, 2, P])
    cmp_b = const("cmp_b", [P, 2, 32, NCMP])
    cmp_h = const("cmp_h", [P, 2, NCMP])
    k_cmp = at("k_cmp", [NCMP, HD], F32, MG0 + 6 * KB)
    v_cmp = at("v_cmp", [NCMP, HD], F32, MG0 + 6 * KB + 512)
    k_sq = at("k_sq", [NCMP, HD], F32, MG0 + 7 * KB)
    kt_cmp = at("kt_cmp", [P, NCMP], F32, MG0 + 7 * KB + 512)
    stick_z = [at(f"stick_z{u}", [P, 2, 2, S], F32, XT0 + (8 + 12 * u) * KB) for u in range(2)]
    stick_e = [at(f"stick_e{u}", [P, 2, 2, S], F32, XT0 + (12 + 12 * u) * KB) for u in range(2)]
    stick_l = [at(f"stick_l{u}", [P, 2, 2, S], F32, XT0 + (16 + 12 * u) * KB) for u in range(2)]
    strict = at("strict", [P, 2, S], F32, XT0 + 32 * KB)
    tri = at("tri", [P, 2, P], F32, XT0 + 34 * KB)

    x2_hi = at("x2_hi", [P, NX2, S], F32R, PJ0)
    x2_lo = at("x2_lo", [P, NX2, S], F32R, PJ0 + NX2 * KB)
    x3_hi = at("x3_hi", [P, KT - NX2, S], F32R, XT0 + 40 * KB)
    x3_lo = at("x3_lo", [P, KT - NX2, S], F32R, XT0 + 48 * KB)
    cursor[0] = PJ0 + 2 * NX2 * KB
    key_v = const("key_v", [P, NT, PH, 2, PK])
    key_i = const("key_i", [P, NT, PH, 2, PK], U32)
    pair_v = const("pair_v", [P, NT, PH, PK])
    pair_i = const("pair_i", [P, NT, PH, PK], U32)
    cand = const("cand", [P, PK, PK])
    key_w = const("key_w", [P, 64])
    key_f = const("key_f", [P, 2, PK])
    pair_n = const("pair_n", [P, 2, PK], U32)
    pair_f = const("pair_f", [P, 2, PK])
    picks = const("picks", [P, NT, 3, PH, PK])
    pick_n = const("pick_n", [P, 2, PK], U32)
    iotas = const("iotas", [P, P])
    square = at("square", [P, D], F32, XT0)
    peer_q = at("peer_q", [P, NT, PH * HD], F32, XT0)
    peer_qt = at("peer_qt", [P, PH, S], F32, XT0 + 8 * KB)
    subkeys = at("subkeys", [P, PH, P], F32, XT0 + 16 * KB)
    act_t = at("act_t", [P, KT, S], F32, XT0)
    key_s = at("key_s", [P, NT, PH, 2, 64], F32, XT0 + 32 * KB)
    act_buf = at("act_buf", [P, 2, NT, 512], F32, XT0 + 56 * KB)
    T0 = PJ0 + 2 * NX2 * KB
    kmaj = at("kmaj", [P, 3, S], F32, T0)
    hot_q = at("hot_q", [P, 3, HOT, 32], F32, T0 + 3 * KB)
    hot_c = [at(f"hot_c{i}", [P, HOT, P], F32, off)
             for i, off in enumerate((XT0 + 32 * KB, XT0 + 36 * KB, T0 + 6 * KB))]
    wmat = at("wmat", [P, KT, S], F32, MG0)
    h_rows = at("h_rows", [P, NT, D], F32, PJ0)

    used = [0]

    def piece(n, parts=P):
        used[0] += n
        return small[0:parts, used[0] - n:used[0]]

    rstd_x, ms_x, ms_h, rstd_h = piece(2), piece(4), piece(4), piece(2)
    head_ms = {(b, h): piece(8) for b in "bcd" for h in range(NT)}
    head_rstd = {(b, h): piece(8) for b in "bcd" for h in range(NT)}
    half_exp = piece(8)
    row_max, row_neg, row_den, row_inv = piece(6), piece(6), piece(6), piece(6)
    nsa_gate, top8, k_ms, k_rstd = piece(24), piece(8), piece(1, NCMP), piece(1, NCMP)
    soft_den, soft_inv = piece(16), piece(16)

    acc = nc.alloc_psum_tensor("acc", [P, 2, NT, 512], F32)
    side = nc.alloc_psum_tensor("side", [P, 4, 512], F32)

    def sems(*names):
        return [nc.alloc_semaphore(n) for n in names]

    raw_loaded = sems(*(f"raw_loaded{i}" for i in range(RING)))
    hi_ready, lo_ready, chunk_used = sems("hi_ready", "lo_ready", "chunk_used")
    lo_shared = nc.alloc_semaphore("lo_shared")
    bank_free = sems("bank_free0", "bank_free1")
    xt_loaded = sems(*(f"xt_loaded{i}" for i in range(4)))
    g_mix_loaded, ident_loaded, attn_loaded, rows_loaded, x_loaded, cmp_loaded = sems(
        "g_mix_loaded", "ident_loaded", "attn_loaded", "rows_loaded", "x_loaded", "cmp_loaded")
    stick_loaded, subkeys_loaded, iotas_loaded, stored = sems(
        "stick_loaded", "subkeys_loaded", "iotas_loaded", "stored")
    xt_hi_done, xt_lo_done, xt_turned = sems("xt_hi_done", "xt_lo_done", "xt_turned")
    squares_done, rstd_ready, half_ready = sems("squares_done", "rstd_ready", "half_ready")
    head_ms_done, head_rstd_done, heads_ready = sems("head_ms_done", "head_rstd_done", "heads_ready")
    turned, turned_copied = sems("turned", "turned_copied")
    z_turned, z_hi_done, z_lo_done = sems("z_turned", "z_hi_done", "z_lo_done")
    index_ready, index_read, nsa_gate_ready = sems("index_ready", "index_read", "nsa_gate_ready")
    scores_ready, row_max_ready, exp_ready = sems("scores_ready", "row_max_ready", "exp_ready")
    probs_ready, probs_turned, probs_copied = sems("probs_ready", "probs_turned", "probs_copied")
    pv_done, out_hi_done, out_lo_done = sems("pv_done", "out_hi_done", "out_lo_done")
    cmp_blocks, cmp_hidden, cmp_act, cmp_out = sems("cmp_blocks", "cmp_hidden", "cmp_act", "cmp_out")
    cmp_square, cmp_rstd, cmp_normed, cmp_turned, cmp_ready = sems(
        "cmp_square", "cmp_rstd", "cmp_normed", "cmp_turned", "cmp_ready")
    stick_scores, stick_soft, stick_masked = sems("stick_scores", "stick_soft", "stick_masked")
    stick_sums, stick_arg, stick_exp, stick_weights = sems("stick_sums", "stick_arg", "stick_exp", "stick_weights")
    stick_out, stick_hi, stick_lo = sems("stick_out", "stick_hi", "stick_lo")
    gate_used, pq_turned, pq_copied = sems("gate_used", "pq_turned", "pq_copied")
    key_scores, picks_shifted, picks_exp = sems("key_scores", "picks_shifted", "picks_exp")
    picks_ready, picks_turned, picks_copied = sems("picks_ready", "picks_turned", "picks_copied")
    act_turned, act_copied = sems("act_turned", "act_copied")
    hot_c_ready = sems("hot_c_ready0", "hot_c_ready1")
    h_stored, h_loaded, gates_put = sems("h_stored", "h_loaded", "gates_put")
    hot_distance, hot_q_ready, scattered = sems("hot_distance", "hot_q_ready", "scattered")
    wmat_ready, wmat_hi, wmat_lo = sems("wmat_ready", "wmat_hi", "wmat_lo")
    dve_chain, act_chain, pool_chain = sems("dve_chain", "act_chain", "pool_chain")

    def chain(eng, own):
        count = [0]

        def then(instruction):
            count[0] += 1
            instruction.then_inc(own, 1)
            eng.wait_ge(own, count[0])
        return then

    def tile_rows(h):
        return slice(h * P, (h + 1) * P)

    def flat(ap):
        return ap.rearrange("p a b -> p (a b)")

    def evacuated(eng, group):
        eng.wait_ge(bank_free[group % 2], group // 2 + 1)
        if group:
            eng.wait_ge(bank_free[(group - 1) % 2], (group - 1) // 2 + 1)

    def mix_place(slot):
        for b in MERGE:
            per = 1 + MIX_K[b] // 2
            if MIX_CH[b] <= slot < MIX_CH[b] + GRP * per:
                return b, (slot - MIX_CH[b]) // per, (slot - MIX_CH[b]) % per

    def mix_end(b, n):
        return MIX_CH[b] + (n + 1) * (1 + MIX_K[b] // 2) - 1

    MIX_OUT = {mix_end(b, n) + LEAD: (b, n) for b in MERGE for n in range(GRP)}
    GATE_OUT = {MIX_CH[b] + n * (1 + MIX_K[b] // 2) + LEAD: (b, n) for b in MERGE for n in range(GRP)}
    OUT_OUT = {CH_OUT + (n + 1) * CPG + LEAD: n for n in range(GRP)}
    XT_TURN = {}
    for n in range(GRP):
        for j in range(2):
            XT_TURN[mix_end("a", n) + LEAD + 2 + j] = 2 * n + j
            h_slot = CH_WQ if n == NX2 // 4 else CH_OUT + (n + 1) * CPG + LEAD + 2
            XT_TURN[h_slot + j] = 2 * GRP + 2 * n + j

    with nc.Block() as block:

        @block.sync
        def _(sp):
            def load(src, slot, width, used_by=None):
                if used_by is not None:
                    sp.wait_ge(lo_ready, used_by)
                sp.dma_start(w_raw[:, slot, 0:width], src).then_inc(raw_loaded[slot], 16)

            for c in range(RING):
                load(io["w_in"][c], c, 2 * W1C)
            with sp.Fori(1, CH_MIX // RING) as g:
                for c in range(RING):
                    load(io["w_in"][bass.ds(g * RING + c, 1)].rearrange("a p n -> (a p) n"), c, 2 * W1C,
                         g * RING + (c - RING + 1))
            with sp.Fori(0, (CH_END - CH_MIX) // RING) as g:
                for c in range(RING):
                    load(io["stream"][bass.ds(g * RING + c, 1)].rearrange("a p n -> (a p) n"), c, 1024,
                         g * RING + (CH_MIX + c - RING + 1))

        @block.tensor
        def _(pe):
            def products(parity, chunk, slot, lhs, k0, width, first, last):
                pe.wait_ge(lo_ready, chunk + 1)
                for j in range(2):
                    wh = w_hi[:, slot, j * width:(j + 1) * width]
                    wl = w_lo[:, slot, j * width:(j + 1) * width]
                    for h in range(NT):
                        o = acc[:, parity, h, 0:width]
                        xh, xl = lhs(k0 + j, h)
                        pe.matmul(o, xh, wh, start=first and j == 0, stop=False)
                        pe.matmul(o, xh, wl, start=False, stop=False)
                        mm = pe.matmul(o, xl, wh, start=False, stop=last and j == 1)
                mm.then_inc(chunk_used, 1)

            def xt(k, h):
                return xt_hi[:, k, tile_rows(h)], xt_lo[:, k, tile_rows(h)]

            def x2(k, h):
                if k < NX2:
                    return x2_hi[:, k, tile_rows(h)], x2_lo[:, k, tile_rows(h)]
                return x3_hi[:, k - NX2, tile_rows(h)], x3_lo[:, k - NX2, tile_rows(h)]

            def by_tile(pair):
                return lambda k, h: (pair[0][:, h, k, :], pair[1][:, h, k, :])

            def bank(parity, uses):
                if not (isinstance(uses, int) and uses == 0):
                    pe.wait_ge(bank_free[parity], uses)

            def turn(n):
                s, b, br, blocks = TURNS[n]
                if br == "i":
                    pe.wait_ge(ident_loaded, 32)
                    evacuated(pe, 2)
                elif br == "a":
                    evacuated(pe, NG1 - 1)
                    pe.wait_ge(probs_copied, len(PASSES))
                    pe.wait_ge(out_lo_done, 6)
                else:
                    pe.wait_ge(heads_ready, "bcd".index(br) * NT + NT)
                before = [m for m in range(n) if TURNS[m][1] == b]
                if before:
                    pe.wait_ge(turned_copied, before[-1] + 1)
                if br == "c":
                    pe.wait_ge(cmp_ready, 1)
                    pe.wait_ge(out_lo_done, 2)
                for i, blk in enumerate(blocks):
                    for h in range(NT):
                        if br == "i":
                            o, c = side[0:64, b, i * S + h * P:i * S + (h + 1) * P], B_IQ + 64 * blk
                            src = proj[:, h, c:c + 64]
                        else:
                            o = side[:, b, i * S + h * P:i * S + (h + 1) * P]
                            c = OUT_COL[br] + blk * HD if (br, blk) != ("b", 6) else B_VC
                            src = proj[:, h, c:c + HD]
                        mm = pe.transpose(o, src, ident[:])
                mm.then_inc(turned, 1)

            def turn_z():
                last = max(n for n, t in enumerate(TURNS) if t[0] < Z_TURN)
                pe.wait_ge(turned_copied, last + 1)
                for h in range(NT):
                    for b in range(2):
                        mm = pe.transpose(side[:, 2, (2 * h + b) * P:(2 * h + b + 1) * P],
                                          proj[:, h, Z_COL + b * P:Z_COL + (b + 1) * P], ident[:])
                mm.then_inc(z_turned, 1)

            def index_scores(h):
                pe.wait_ge(turned_copied, 3)
                if h:
                    pe.wait_ge(index_read, h)
                q = feat["i"]
                for i in range(4):
                    mm = pe.matmul(side[:, i // 2, (i % 2) * S:(i % 2 + 1) * S],
                                   q[:, i, tile_rows(h)], q[:, 4, :], start=True, stop=True)
                mm.then_inc(index_ready, 1)

            def cmp_hidden_part(n):
                w, half = n // 2, n % 2
                if n == 0:
                    pe.wait_ge(cmp_blocks, 1)
                    pe.wait_ge(turned_copied, 7)
                pe.wait_ge(cmp_loaded, 16 * (n + 1))
                for l in range(16):
                    mm = pe.matmul(side[:, 2, w * 32:w * 32 + NCMP], cmp_w1[:, l, :],
                                   cmp_b[:, w, half * 16 + l, :], start=(half == 0 and l == 0),
                                   stop=(half == 1 and l == 15))
                mm.then_inc(cmp_hidden, 1)

            def cmp_second():
                pe.wait_ge(cmp_act, 1)
                for w in range(2):
                    mm = pe.matmul(side[0:NCMP, 2, 128 * (w + 1):128 * (w + 2)], cmp_h[:, w, :], cmp_w2[:, w, :],
                                   start=True, stop=True)
                mm.then_inc(cmp_out, 1)

            def cmp_turn():
                pe.wait_ge(cmp_normed, 1)
                pe.transpose(side[:, 2, 64:64 + NCMP], k_cmp[:], ident[0:NCMP, 0:NCMP]).then_inc(cmp_turned, 1)

            def scores(i):
                br, h, part = PASSES[i]
                if i:
                    pe.wait_ge(probs_copied, i)
                else:
                    pe.wait_ge(index_read, 2)
                need = {"b": 7, "c": 10, "d": 14}[br]
                pe.wait_ge(turned_copied, need)
                f = feat[br]
                if br == "b":
                    pairs = [(r, f[:, 4, :]) for r in range(4)]
                elif br == "c":
                    pe.wait_ge(cmp_ready, 1)
                    key = (kt_cmp[:], f[:, 4, :], f[:, 5, :])[part]
                    pairs = [(r, key) for r in range(4)]
                else:
                    pe.wait_ge(z_lo_done, 1)
                    pairs = [(2 * g + s, f[:, 6 + s, :]) for s in range(2) for g in range(3)]
                nk = NCMP if (br, part) == ("c", 0) else S
                for r, (q, key) in enumerate(pairs):
                    mm = pe.matmul(side[:, r // 2, (r % 2) * S:(r % 2) * S + nk], f[:, q, tile_rows(h)], key,
                                   start=True, stop=True)
                mm.then_inc(scores_ready, 1)

            def turn_probs(i):
                br, h, part = PASSES[i]
                nk = NCMP if (br, part) == ("c", 0) else S
                pe.wait_ge(probs_ready, i + 1)
                for s in range(1 if nk == NCMP else 2):
                    for r in range(2 if br == "d" else 4):
                        mm = pe.transpose(side[0:min(nk, P), s, r * P:(r + 1) * P],
                                          probs[:, 3 * r if br == "d" else r, s * P:min((s + 1) * P, nk)], ident[:])
                mm.then_inc(probs_turned, 1)

            def weigh_values(i):
                br, h, part = PASSES[i]
                pe.wait_ge(probs_copied, i + 1)
                if first_part(br, part):
                    done = sum(last_part(p[0], p[2]) for p in PASSES[:i])
                    if done:
                        pe.wait_ge(out_lo_done, done)
                    if br == "c":
                        pe.wait_ge(turned_copied, 10)
                if (br, part) == ("c", 0):
                    mm = pe.matmul(side[:, 3, :], v_cmp[:], probs_t[0:NCMP, 0, :, :], start=False, stop=True)
                elif br == "d":
                    for hs in range(2):
                        for s in range(2):
                            mm = pe.matmul(side[:, 3, hs * P:(hs + 1) * P],
                                           proj[:, s, D_V + hs * HD:D_V + (hs + 1) * HD],
                                           probs_t[:, s, hs, :], start=(s == 0), stop=(s == 1))
                else:
                    col = {("b", 0): B_V, ("c", 1): C_VS, ("c", 2): C_VW}[br, part]
                    for s in range(2):
                        mm = pe.matmul(side[:, 3, :], proj[:, s, col:col + HD], probs_t[:, s, :, :],
                                       start=(s == 0 and first_part(br, part)), stop=(s == 1 and last_part(br, part)))
                mm.then_inc(pv_done, 1)

            def stick_z_scores(u):
                pe.wait_ge(turned_copied, len(TURNS))
                if u:
                    pe.wait_ge(stick_lo, 1)
                for r in range(2):
                    for s in range(2):
                        mm = pe.matmul(side[:, r, s * S:(s + 1) * S],
                                       feat["a"][:, 4 + 2 * u + r, tile_rows(s)], feat["a"][:, 2 * u + r, :],
                                       start=True, stop=True)
                mm.then_inc(stick_scores, 1)

            def stick_cumulate(u):
                pe.wait_ge(stick_loaded, 32)
                pe.wait_ge(stick_masked, u + 1)
                for r in range(2):
                    pe.matmul(side[:, 2 + r, 0:S], tri[:, 0, :], stick_l[u][:, r, 0, :], start=True, stop=False)
                    pe.matmul(side[:, 2 + r, 0:S], tri[:, 1, :], stick_l[u][:, r, 1, :], start=False, stop=True)
                    mm = pe.matmul(side[:, 2 + r, S:2 * S], tri[:, 0, :], stick_l[u][:, r, 1, :], start=True, stop=True)
                mm.then_inc(stick_sums, 1)

            def stick_values(u):
                pe.wait_ge(stick_weights, u + 1)
                for r in range(2):
                    for s in range(2):
                        col = A_V + (2 * u + r) * HD
                        mm = pe.matmul(side[:, 0, r * S:(r + 1) * S], proj[:, s, col:col + HD],
                                       stick_e[u][:, r, s, :], start=(s == 0), stop=(s == 1))
                mm.then_inc(stick_out, 1)

            def turn_rows(q):
                if q < KT // 2:
                    pe.wait_ge(gate_used, 3 * GRP + q // 2 + 1)
                    if q < 4:
                        pe.wait_ge(stick_lo, 2)
                else:
                    evacuated(pe, GN_OUT + (q - KT // 2) // 2)
                if q >= 4:
                    pe.wait_ge(xt_lo_done, KT + q - 3)
                k = 2 * (q % (KT // 2))
                for j in range(2):
                    for h in range(NT):
                        mm = pe.transpose(side[:, q % 4, j * S + h * P:j * S + (h + 1) * P],
                                          rows[:, h, (k + j) * P:(k + j + 1) * P], ident[:])
                mm.then_inc(xt_turned, 1)

            def turn_queries(n):
                evacuated(pe, GN_WQ + n // 2)
                pe.wait_ge(xt_lo_done, 2 * KT)
                for r in range(2):
                    for h in range(NT):
                        mm = pe.transpose(side[:, n, r * S + h * P:r * S + (h + 1) * P],
                                          peer_q[:, h, (2 * n + r) * HD:(2 * n + r + 1) * HD], ident[:])
                mm.then_inc(pq_turned, 1)

            def score_keys(n):
                pe.wait_ge(subkeys_loaded, 16)
                pe.wait_ge(pq_copied, 2 * n + 2)
                for h in range(NT):
                    for r in range(4):
                        mm = pe.matmul(side[:, 2 * n + h, r * P:(r + 1) * P],
                                       peer_qt[:, 4 * n + r, tile_rows(h)], subkeys[:, 4 * n + r, :],
                                       start=True, stop=True)
                mm.then_inc(key_scores, 1)

            def turn_act(t):
                gn = GN_U + t
                pe.wait_ge(bank_free[gn % 2], gn // 2 + 1)
                for j in range(2):
                    pe.wait_ge(act_copied, 2 * t + 3 + j)
                    for i in range(2):
                        for h in range(NT):
                            k = 2 * j + i
                            mm = pe.transpose(side[:, 2 + j, i * S + h * P:i * S + (h + 1) * P],
                                              act_buf[:, t % 2, h, k * P:(k + 1) * P], ident[:])
                    mm.then_inc(act_turned, 1)

            def turn_picks():
                pe.wait_ge(picks_ready, 1)
                pe.wait_ge(act_copied, 2)
                for h in range(NT):
                    for c in range(3):
                        mm = pe.transpose(side[:, h, c * P:(c + 1) * P],
                                          picks[:, h, c, :, :].rearrange("p a b -> p (a b)"), ident[:])
                mm.then_inc(picks_turned, 1)

            def scatter(n):
                pe.wait_ge(picks_copied, 1)
                pe.wait_ge(hot_c_ready[n % 2], n // 2 + 1)
                pe.wait_ge(hot_q_ready, n + 1)
                if n >= 2:
                    pe.wait_ge(gates_put, n - 1)
                for t in range(HOT):
                    mm = pe.matmul(side[:, n % 2, t * 32:(t + 1) * 32], hot_c[n % 3][:, t, :], hot_q[:, n % 3, t, :],
                                   start=True, stop=True)
                mm.then_inc(scattered, 1)

            def between(s):
                for n, t in enumerate(TURNS):
                    if t[0] == s:
                        turn(n)
                if s == Z_TURN:
                    turn_z()
                if s in INDEX_AT:
                    index_scores(INDEX_AT.index(s))
                if s in CMP_HID:
                    cmp_hidden_part(CMP_HID.index(s))
                if s == CMP_OUT:
                    cmp_second()
                if s == CMP_OUT + 6:
                    cmp_turn()
                for i, at_slot in enumerate(PASS_AT):
                    if s == at_slot:
                        scores(i)
                    if s == at_slot + 5:
                        turn_probs(i)
                    if s == at_slot + 7:
                        weigh_values(i)
                for u, at_slot in enumerate(STICK_AT):
                    if s == at_slot:
                        stick_z_scores(u)
                    if s == at_slot + 9:
                        stick_cumulate(u)
                    if s == at_slot + 16:
                        stick_values(u)
                if s in XT_TURN:
                    turn_rows(XT_TURN[s])
                for n in range(4):
                    if s == CH_WQ + CPG * (n // 2 + 1) + LEAD + 2 + n % 2:
                        turn_queries(n)
                for n in range(2):
                    if s == CH_WQ + CPG * (n + 1) + LEAD + 7:
                        score_keys(n)
                if (s - CH_U) % CPG == LEAD + 2 and s > CH_U + CPG:
                    turn_act((s - CH_U) // CPG - 1)
                if s == PICKS_TURN:
                    turn_picks()
                if SCATTER_AT <= s < SCATTER_AT + ROUNDS:
                    scatter(s - SCATTER_AT)

            for s in range(CH_MIX):
                g, c = s // CPG, s % CPG
                if c == 0:
                    bank(g % 2, g // 2)
                if g == 0:
                    pe.wait_ge(xt_lo_done, 2 * c + 2)
                products(g % 2, s, s % RING, xt, 2 * c, W1C, c == 0, c == CPG - 1)
                between(s)
            for s in range(CH_MIX, CH_OUT):
                b, n, j = mix_place(s)
                before = MERGE.index(b) * GRP + n
                if j == 0:
                    bank(1, GN_MIX // 2 + before)
                    if s == CH_MIX:
                        pe.wait_ge(z_lo_done, 1)
                    products(1, s, s % RING, by_tile(zt), 0, 512, True, True)
                else:
                    if j == 1:
                        bank(0, (GN_MIX + 1) // 2 + before)
                    if n == 0 and j == 1:
                        pe.wait_ge(out_lo_done, {"b": 2, "c": 4, "d": 6, "a": 6}[b])
                        if b == "a":
                            pe.wait_ge(stick_lo, 2)
                    products(0, s, s % RING, by_tile(ot[b]), 2 * (j - 1), 512, j == 1, j == MIX_K[b] // 2)
                between(s)
            for s in range(CH_OUT, CH_V):
                g, c = (s - CH_OUT) // CPG, (s - CH_OUT) % CPG
                gn = GN_OUT + g
                if c == 0:
                    bank(gn % 2, gn // 2)
                if g in (0, GRP):
                    base_q = 0 if g == 0 else KT // 2
                    pe.wait_ge(xt_lo_done, KT + base_q + c + 1)
                products(gn % 2, s, s % RING, xt if s < CH_WQ else x2, 2 * c, 512, c == 0, c == CPG - 1)
                between(s)
            for s in range(CH_V, CH_V + CPG):
                c = s - CH_V
                if c == 0:
                    bank(GN_V % 2, GN_V // 2)
                pe.wait_ge(wmat_lo, c + 1)
                products(GN_V % 2, s, s % RING, xt, 2 * c, 512, c == 0, c == CPG - 1)
                between(s)

            def outputs(m, k):
                gn = GN_V + k
                bank(gn % 2, m + gn // 2)
                for c in range(CPG):
                    products(gn % 2, m * (2 * CPG) + (CH_V + k * CPG + c), c % RING, xt, 2 * c, 512,
                             c == 0, c == CPG - 1)

            outputs(0, 1)
            with pe.Fori(1, GRP // 2) as m:
                for k in range(2):
                    outputs(m, k)

        @block.scalar
        def _(act):
            then = chain(act, act_chain)
            act.dma_start(g_mix[:], io["g_mix"]).then_inc(g_mix_loaded, 16)
            for i in range(4):
                act.dma_start(xt_raw[:, 8 * i:8 * i + 8, :], io["xt"][:, 8 * i:8 * i + 8, :]).then_inc(xt_loaded[i], 16)
            act.dma_start(ident[:], io["ident"]).then_inc(ident_loaded, 16)
            act.dma_start(g_ffn[:], io["g_ffn"]).then_inc(ident_loaded, 16)
            for name, t in (("causal", causal), ("dil", dil), ("rope", rope), ("gains", gains),
                            ("cmp_mask", cmp_mask), ("pe_t", pe_t), ("cmp_w2", cmp_w2)):
                act.dma_start(t[:], io[name]).then_inc(attn_loaded, 16)

            def hi(chunk, slot, width, m4):
                act.wait_ge(raw_loaded[slot], m4 * 16 + 16)
                if not (isinstance(chunk, int) and chunk < RING):
                    act.wait_ge(chunk_used, chunk - (RING - 1))
                nc.scalar.activation(w_hi[:, slot, 0:width], w_raw[:, slot, 0:width], ACT.Copy).then_inc(hi_ready, 1)

            def squares(i, ms):
                h, half = i // 2, slice((i % 2) * 2048, (i % 2) * 2048 + 2048)
                if ms is ms_x:
                    act.wait_ge(rows_loaded, 16)
                    out = rows[:, h, half]
                else:
                    evacuated(act, GN_WQ - 1)
                    if i > 1:
                        act.wait_ge(squares_done, 4 + i - 1)
                    out = square[:, half]
                nc.scalar.activation(out, rows[:, h, half], ACT.Square, accum_out=ms[:, i:i + 1])\
                    .then_inc(squares_done, 1)

            def evacuate_in(g):
                act.wait_ge(chunk_used, g * CPG + CPG)
                act.wait_ge(rstd_ready, 1)
                for h in range(NT):
                    e = nc.scalar.activation(proj[:, h, g * W1C:(g + 1) * W1C], acc[:, g % 2, h, 0:W1C],
                                             ACT.Copy, scale=rstd_x[:, h:h + 1])
                e.then_inc(bank_free[g % 2], 1)

            def copy_turned(n):
                _, b, br, blocks = TURNS[n]
                act.wait_ge(turned, n + 1)
                parts, w = 64 if br == "i" else P, len(blocks) * S
                nc.scalar.activation(flat(feat[br][0:parts, blocks[0]:blocks[-1] + 1, :]), side[0:parts, b, 0:w],
                                     ACT.Copy).then_inc(turned_copied, 1)

            def z_hi():
                act.wait_ge(z_turned, 1)
                nc.scalar.activation(zt[0][:].rearrange("p a b c -> p (a b c)"), side[:, 2, :], ACT.Copy)\
                    .then_inc(z_hi_done, 1)

            def nsa_gates():
                evacuated(act, 2)
                act.wait_ge(attn_loaded, 112)
                nc.scalar.activation(nsa_gate.rearrange("p (a b) -> p a b", b=12), proj[:, :, B_CG:B_CG + 12],
                                     ACT.Sigmoid).then_inc(nsa_gate_ready, 1)

            def load_cmp(n):
                if n:
                    act.wait_ge(cmp_hidden, n)
                else:
                    act.wait_ge(bank_free[0], 1)
                act.dma_start(cmp_w1[:], io["cmp_w1"][n // 2][:, 16 * (n % 2):16 * (n % 2) + 16, :])\
                    .then_inc(cmp_loaded, 16)

            def cmp_gelu():
                act.wait_ge(cmp_hidden, 4)
                nc.scalar.activation(cmp_h[:], side[:, 2, 0:64].rearrange("p (w n) -> p w n", n=32)[:, :, 0:NCMP],
                                     ACT.Gelu_apprx_tanh).then_inc(cmp_act, 1)

            def exponentials(i):
                br, h, part = PASSES[i]
                nk = NCMP if (br, part) == ("c", 0) else S
                act.wait_ge(row_max_ready, i + 1)
                for r in range(6 if br == "d" else 4):
                    m = r // 3 if br == "d" else r
                    e = nc.scalar.activation(probs[:, r, 0:nk], probs[:, r, 0:nk], ACT.Exp,
                                             bias=row_neg[:, m:m + 1], accum_out=row_den[:, r:r + 1])
                e.then_inc(exp_ready, 1)

            def copy_probs(i):
                br, h, part = PASSES[i]
                heads = 2 if br == "d" else 4
                act.wait_ge(probs_turned, i + 1)
                if i:
                    act.wait_ge(pv_done, i)
                if (br, part) == ("c", 0):
                    e = nc.scalar.activation(flat(probs_t[0:NCMP, 0, :, :]), side[0:NCMP, 0, :], ACT.Copy)
                else:
                    for s in range(2):
                        e = nc.scalar.activation(flat(probs_t[:, s, 0:heads, :]), side[:, s, 0:heads * P], ACT.Copy)
                e.then_inc(probs_copied, 1)

            def out_hi(i):
                br, h, part = PASSES[i]
                act.wait_ge(pv_done, i + 1)
                nc.scalar.activation(flat(ot[br][0][:, h]), side[:, 3, 0:MIX_K[br] * P], ACT.Copy)\
                    .then_inc(out_hi_done, 1)

            def stick_flat(t):
                return t[:].rearrange("p a b c -> p (a b c)")

            def stick_scale(u):
                act.wait_ge(stick_scores, u + 1)
                then(nc.scalar.activation(stick_flat(stick_z[u]), flat(side[:, 0:2, :]), ACT.Copy, scale=SCALE))
                then(nc.scalar.activation(stick_flat(stick_l[u]), stick_flat(stick_z[u]), ACT.Abs))

            def stick_softplus(u):
                z = stick_flat(stick_l[u])
                then(nc.scalar.activation(z, z, ACT.Exp, scale=-1.0))
                nc.scalar.activation(z, z, ACT.Ln, bias=1.0).then_inc(stick_soft, 1)

            def stick_exps(u):
                act.wait_ge(stick_arg, u + 1)
                nc.scalar.activation(stick_flat(stick_e[u]), stick_flat(stick_e[u]), ACT.Exp).then_inc(stick_exp, 1)

            def stick_out_hi(u):
                act.wait_ge(stick_out, u + 1)
                nc.scalar.activation(ot["a"][0][:, :, 2 * u:2 * u + 2, :],
                                     side[:, 0, :].rearrange("p (r h t) -> p h r t", r=2, h=NT), ACT.Copy)\
                    .then_inc(stick_hi, 1)

            def gates(s, b, n):
                before = MERGE.index(b) * GRP + n
                act.wait_ge(chunk_used, s - LEAD + 1)
                if before >= 2:
                    act.wait_ge(gate_used, before - 1)
                for h in range(NT):
                    e = nc.scalar.activation(gate[:, n % 2, h, :], acc[:, 1, h, :], ACT.Sigmoid)
                e.then_inc(bank_free[1], 1)

            def rows_hi(q):
                act.wait_ge(xt_turned, q + 1)
                k = 2 * (q % (KT // 2))
                if q < KT // 2:
                    e = nc.scalar.activation(flat(xt_hi[:, k:k + 2, :]), side[:, q % 4, :], ACT.Copy)
                else:
                    for j in range(2):
                        dst = x2_hi[:, k + j, :] if k < NX2 else x3_hi[:, k + j - NX2, :]
                        e = nc.scalar.activation(dst, side[:, q % 4, j * S:(j + 1) * S], ACT.Copy,
                                                 scale=g_ffn[:, k + j:k + j + 1])
                e.then_inc(xt_hi_done, 1)

            def queries(n):
                gn = GN_WQ + n
                act.wait_ge(rstd_ready, 2)
                act.wait_ge(chunk_used, CH_WQ + (n + 1) * CPG)
                for h in range(NT):
                    e = nc.scalar.activation(peer_q[:, h, n * 512:(n + 1) * 512], acc[:, gn % 2, h, :], ACT.Copy,
                                             scale=rstd_h[:, h:h + 1])
                e.then_inc(bank_free[gn % 2], 1)

            def copy_queries(n):
                act.wait_ge(pq_turned, n + 1)
                nc.scalar.activation(flat(peer_qt[:, 2 * n:2 * n + 2, :]), side[:, n, :], ACT.Copy)\
                    .then_inc(pq_copied, 1)

            def copy_keys(n):
                act.wait_ge(key_scores, n + 1)
                for h in range(NT):
                    nc.scalar.activation(key_s[:, h, 4 * n:4 * n + 4].rearrange("p a b c -> p (a b c)"),
                                         side[:, 2 * n + h, :], ACT.Copy).then_inc(act_copied, 1)

            def picks_exps():
                act.wait_ge(picks_shifted, 1)
                p = pair_v[:].rearrange("p a b c -> p (a b c)")
                nc.scalar.activation(p, p, ACT.Exp).then_inc(picks_exp, 1)

            def put_act(g):
                act.wait_ge(chunk_used, CH_U + (g + 1) * CPG)
                if g >= 2:
                    act.wait_ge(act_turned, 2 * g - 2)
                for h in range(NT):
                    e = nc.scalar.activation(act_buf[:, g % 2, h, :], acc[:, (GN_U + g) % 2, h, :],
                                             ACT.Gelu_apprx_tanh, scale=rstd_h[:, h:h + 1])
                e.then_inc(bank_free[(GN_U + g) % 2], 1)

            def copy_act(t):
                for j in range(2):
                    act.wait_ge(act_turned, 2 * t + j + 1)
                    k = 4 * t + 2 * j
                    nc.scalar.activation(flat(act_t[:, k:k + 2, :]), side[:, 2 + j, :], ACT.Copy)\
                        .then_inc(act_copied, 1)

            def one_hot(n):
                act.wait_ge(hot_distance, n // 2 + 1)
                d = flat(hot_c[n % 3][:])
                then(nc.scalar.activation(d, d, ACT.Abs))
                nc.scalar.activation(d, d, ACT.Relu, scale=-1.0, bias=1.0).then_inc(hot_c_ready[1], 1)

            def put_gates(n):
                act.wait_ge(scattered, n + 1)
                if n == 0:
                    act.wait_ge(h_stored, 32)
                nc.scalar.activation(wmat[:, :, n * HOT:(n + 1) * HOT],
                                     side[:, n % 2, 0:HOT * 32].rearrange("p (t q) -> p q t", q=32), ACT.Copy)\
                    .then_inc(gates_put, 1)

            def wmat_hi_part(q):
                act.wait_ge(wmat_ready, q + 1)
                nc.scalar.activation(flat(xt_hi[:, 2 * q:2 * q + 2, :]), flat(wmat[:, 2 * q:2 * q + 2, :]), ACT.Copy)\
                    .then_inc(wmat_hi, 1)

            def between(s):
                if s == RING:
                    act.wait_ge(xt_lo_done, KT)
                    act.dma_start(rows[:], io["x"]).then_inc(rows_loaded, 16)
                for at_slot, ms in ((SQUARES_X, ms_x), (SQUARES_H, ms_h)):
                    if at_slot <= s < at_slot + 4:
                        squares(s - at_slot, ms)
                if s % CPG == LEAD and 1 <= s // CPG <= NG1:
                    evacuate_in(s // CPG - 1)
                for n, t in enumerate(TURNS):
                    if s == t[0] + LEAD:
                        copy_turned(n)
                if s == Z_TURN + LEAD:
                    z_hi()
                if s == B_READY + 2:
                    nsa_gates()
                if s in CMP_LOAD:
                    load_cmp(CMP_LOAD.index(s))
                if s == CMP_HID[-1] + LEAD:
                    cmp_gelu()
                for i, at_slot in enumerate(PASS_AT):
                    if s == at_slot + 4:
                        exponentials(i)
                    if s == at_slot + 8:
                        copy_probs(i)
                    if s == at_slot + 10 and last_part(PASSES[i][0], PASSES[i][2]):
                        out_hi(i)
                for u, at_slot in enumerate(STICK_AT):
                    if s == at_slot + 3:
                        stick_scale(u)
                    if s == at_slot + 4:
                        stick_softplus(u)
                    if s == at_slot + 13:
                        stick_exps(u)
                    if s == at_slot + 19:
                        stick_out_hi(u)
                if s in GATE_OUT:
                    gates(s, *GATE_OUT[s])
                if s - LEAD in XT_TURN:
                    rows_hi(XT_TURN[s - LEAD])
                for n in range(2):
                    if s == CH_WQ + CPG * (n + 1) + LEAD:
                        queries(n)
                    if s == CH_WQ + CPG * (n + 1) + LEAD + 10:
                        copy_keys(n)
                for n in range(4):
                    if s == CH_WQ + CPG * (n // 2 + 1) + 2 * LEAD + 2 + n % 2:
                        copy_queries(n)
                if s >= CH_U + CPG and (s - CH_U) % CPG == LEAD:
                    put_act((s - CH_U) // CPG - 1)
                if s > CH_U + CPG and (s - CH_U) % CPG == 2 * LEAD + 2:
                    copy_act((s - CH_U) // CPG - 1)
                if s == SOFTMAX_AT + 1:
                    picks_exps()
                n = s - SCATTER_AT - 3
                if 0 <= n < ROUNDS:
                    put_gates(n)
                if 0 <= n + 1 < ROUNDS and n % 2 == 0:
                    one_hot(n + 1)
                if 0 <= s - CH_V < KT // 2:
                    wmat_hi_part(s - CH_V)

            act.wait_ge(g_mix_loaded, 16)
            for k in range(KT):
                if k % 8 == 0:
                    act.wait_ge(xt_loaded[k // 8], 16)
                nc.scalar.activation(xt_hi[:, k, :], xt_raw[:, k, :], ACT.Copy, scale=g_mix[:, k:k + 1])\
                    .then_inc(xt_hi_done, 1)
                if k % 2 and k // 2 < RING:
                    hi(k // 2, k // 2, 2 * W1C, 0)
            for s in range(RING, CH_V + CPG):
                hi(s, s % RING, 2 * W1C if s < CH_MIX else 1024, s // RING)
                between(s)

            with act.Fori(1, GRP) as m:
                for c in range(CPG):
                    hi(m * CPG + (CH_V + c), c % RING, 1024, m * (CPG // RING) + (CH_V // RING + c // RING))

        @block.vector
        def _(dve):
            then = chain(dve, dve_chain)

            def lo(chunk, slot, width):
                dve.wait_ge(hi_ready, chunk + 1)
                nc.vector.tensor_tensor(w_lo[:, slot, 0:width], w_raw[:, slot, 0:width],
                                        w_hi[:, slot, 0:width].bitcast(F32), ALU.subtract).then_inc(lo_ready, 1)

            def los(base_chunk, c0, c1, width=1024):
                for c in range(c0, c1):
                    lo(base_chunk + c, c % RING, width)

            def norm_piece(br, i):
                c0, roped_n, normed, spans = HEADS[br]
                h = i % 2 if i < 4 else (i - 4) // 2
                n = "bcd".index(br) * NT + h
                ms, rstd = head_ms[br, h][:, 0:normed], head_rstd[br, h][:, 0:normed]
                heads = proj[:, h, c0:c0 + normed * HD].rearrange("p (a b) -> p a b", b=HD)
                roped = proj[:, h, c0:c0 + roped_n * HD].rearrange("p (a b) -> p a b", b=HD)
                if i < 2:
                    evacuated(dve, {"b": 2, "c": 4, "d": 7}[br])
                    dve.wait_ge(attn_loaded, 112)
                    tmp = rope_tmp[:, 0:normed * HD].rearrange("p (a b) -> p a b", b=HD)
                    if n:
                        dve.wait_ge(head_ms_done, n)
                    then(nc.vector.tensor_tensor(tmp, heads, heads, ALU.mult))
                    nc.vector.tensor_reduce(ms, tmp, AX, ALU.add).then_inc(head_ms_done, 1)
                elif i < 4:
                    dve.wait_ge(head_ms_done, n + 1)
                    dve.wait_ge(head_rstd_done, n + 1)
                    then(nc.vector.tensor_tensor(heads, heads, rstd.unsqueeze(2).broadcast_to([P, normed, HD]),
                                                 ALU.mult))
                    for a, b, g in spans:
                        e = nc.vector.tensor_tensor(heads[:, a:b, :], heads[:, a:b, :],
                                                    gains[:, g, :].unsqueeze(1).broadcast_to([P, b - a, HD]), ALU.mult)
                    then(e)
                else:
                    tmp = rope_tmp[:, 0:roped_n * HD].rearrange("p (a b) -> p a b", b=HD)
                    if i % 2 == 0:
                        if h:
                            dve.wait_ge(heads_ready, n)
                        sin = [rope[:, 1 + sign, h, :].unsqueeze(1).broadcast_to([P, roped_n, 64]) for sign in range(2)]
                        nc.vector.tensor_tensor(tmp[:, :, 0:64], roped[:, :, 64:128], sin[1], ALU.mult)
                        then(nc.vector.tensor_tensor(tmp[:, :, 64:128], roped[:, :, 0:64], sin[0], ALU.mult))
                    else:
                        both = proj[:, h, c0:c0 + roped_n * HD].rearrange("p (a b) -> p a b", b=64)
                        cos = rope[:, 0, h, :].unsqueeze(1).broadcast_to([P, 2 * roped_n, 64])
                        then(nc.vector.tensor_tensor(both, both, cos, ALU.mult))
                        nc.vector.tensor_tensor(roped, roped, tmp, ALU.add).then_inc(heads_ready, 1)
                        dve.wait_ge(heads_ready, n + 1)

            def read_index(h):
                dve.wait_ge(index_ready, h + 1)
                for i in range(4):
                    src = side[:, i // 2, (i % 2) * S:(i % 2 + 1) * S]
                    dst = idx_sum if i == 0 else idx_tmp
                    then(nc.vector.tensor_scalar(dst[:], src, 0.0, proj[:, h, B_IW + i:B_IW + i + 1],
                                                 ALU.max, ALU.mult))
                    if i:
                        then(nc.vector.tensor_tensor(idx_sum[:], idx_sum[:], idx_tmp[:], ALU.add))
                dve.nop().then_inc(index_read, 1)
                then(nc.vector.tensor_tensor(idx_sum[:], idx_sum[:], causal[:, h, :], ALU.add))

            def select(h, last):
                for _ in range(2):
                    then(nc.vector.max(top8, idx_sum[:]))
                    then(nc.vector.match_replace(idx_sum[:], top8, idx_sum[:], TAKEN))
                if last:
                    then(nc.vector.tensor_scalar(idx_tmp[:], idx_sum[:], -2e38, NEG, ALU.is_gt, ALU.mult))
                    then(nc.vector.tensor_tensor(sel_mask[:, h, :], idx_tmp[:], causal[:, h, :], ALU.min))

            def compressed_blocks():
                dve.wait_ge(turned_copied, 4)
                for w in range(2):
                    src = feat["b"][:, 5 + w, :].rearrange("p (n l) -> p l n", l=16)
                    for a in range(2):
                        e = nc.vector.tensor_tensor(
                            cmp_b[:, w, a * 16:(a + 1) * 16, :], src[:, :, a:a + NCMP],
                            pe_t[:, w, a * 16:(a + 1) * 16].unsqueeze(2).broadcast_to([P, 16, NCMP]), ALU.add)
                e.then_inc(cmp_blocks, 1)

            def cmp_squares():
                dve.wait_ge(cmp_out, 1)
                then(nc.vector.tensor_copy(k_cmp[:], side[0:NCMP, 2, 128:256]))
                then(nc.vector.tensor_tensor(k_sq[:], k_cmp[:], k_cmp[:], ALU.mult))
                nc.vector.tensor_reduce(k_ms, k_sq[:], AX, ALU.add).then_inc(cmp_square, 1)

            def cmp_norm():
                dve.wait_ge(cmp_rstd, 1)
                nc.vector.scalar_tensor_tensor(out=k_cmp[:], in0=k_cmp[:], scalar=k_rstd, in1=gains[0:NCMP, 3, :],
                                               op0=ALU.mult, op1=ALU.mult).then_inc(cmp_normed, 1)

            def cmp_copy():
                dve.wait_ge(cmp_turned, 1)
                nc.vector.tensor_copy(v_cmp[:], side[0:NCMP, 2, 256:384])
                nc.vector.tensor_copy(kt_cmp[:], side[:, 2, 64:64 + NCMP]).then_inc(cmp_ready, 1)

            def mask_scores(i):
                br, h, part = PASSES[i]
                nk = NCMP if (br, part) == ("c", 0) else S
                heads = 2 if br == "d" else 4
                dve.wait_ge(scores_ready, i + 1)
                if i:
                    dve.wait_ge(probs_turned, i)
                if br == "d":
                    banks = side[:, 0:3, :].rearrange("p a (b c) -> p (a b) c", c=S)
                    for s in range(2):
                        e = nc.vector.scalar_tensor_tensor(
                            out=flat(probs[:, 3 * s:3 * s + 3, :]), in0=flat(banks[:, 3 * s:3 * s + 3, :]),
                            scalar=SCALE, in1=flat(dil[:, h]), op0=ALU.mult, op1=ALU.add)
                    then(e)
                    then(nc.vector.tensor_reduce(row_max[:, 0:2], probs[:].rearrange("p (s g) k -> p s (g k)", g=3),
                                                 AX, ALU.max))
                else:
                    src = side[:, 0:2, :].rearrange("p a (b c) -> p (a b) c", c=S)[:, :, 0:nk]
                    mask = sel_mask[:, h, :] if br == "b" else cmp_mask[:, h, :] if part == 0 else causal[:, h, :]
                    p = probs[:, 0:4, 0:nk]
                    then(nc.vector.scalar_tensor_tensor(
                        out=p, in0=src, scalar=SCALE, in1=mask.unsqueeze(1).broadcast_to([P, 4, nk]),
                        op0=ALU.mult, op1=ALU.add))
                    then(nc.vector.tensor_reduce(row_max[:, 0:4], p, AX, ALU.max))
                nc.vector.tensor_scalar(row_neg[:, 0:heads], row_max[:, 0:heads], -1e37, -1.0, ALU.max, ALU.mult)\
                    .then_inc(row_max_ready, 1)

            def normalise(i):
                br, h, part = PASSES[i]
                nk = NCMP if (br, part) == ("c", 0) else S
                heads = 2 if br == "d" else 4
                dve.wait_ge(exp_ready, i + 1)
                if br == "d":
                    then(nc.vector.tensor_reduce(row_den[:, 0:2], row_den[:, 0:6].rearrange("p (s g) -> p s g", g=3),
                                                 AX, ALU.add))
                then(nc.vector.tensor_scalar(row_den[:, 0:heads], row_den[:, 0:heads], TINY, None, ALU.max))
                then(nc.vector.reciprocal(row_inv[:, 0:heads], row_den[:, 0:heads]))
                if br == "c":
                    dve.wait_ge(nsa_gate_ready, 1)
                    g = nsa_gate[:, h * 12:(h + 1) * 12].rearrange("p (a b) -> p a b", b=3)[:, :, part]
                    then(nc.vector.tensor_tensor(row_inv[:, 0:4], row_inv[:, 0:4], g, ALU.mult))
                if br == "d":
                    sg = probs[:].rearrange("p (s g) k -> p s g k", g=3)
                    then(nc.vector.tensor_tensor(sg[:, :, 0, :], sg[:, :, 0, :], sg[:, :, 1, :], ALU.add))
                    then(nc.vector.tensor_tensor(sg[:, :, 0, :], sg[:, :, 0, :], sg[:, :, 2, :], ALU.add))
                    q = sg[:, :, 0, :]
                else:
                    q = probs[:, 0:4, 0:nk]
                nc.vector.tensor_tensor(q, q, row_inv[:, 0:heads].unsqueeze(2).broadcast_to([P, heads, nk]), ALU.mult)\
                    .then_inc(probs_ready, 1)

            def out_lo(i):
                br, h, part = PASSES[i]
                n = sum(last_part(p[0], p[2]) for p in PASSES[:i + 1])
                dve.wait_ge(out_hi_done, n)
                nc.vector.tensor_tensor(flat(ot[br][1][:, h]), side[:, 3, 0:MIX_K[br] * P],
                                        flat(ot[br][0][:, h]).bitcast(F32), ALU.subtract).then_inc(out_lo_done, 1)

            def z_lo():
                dve.wait_ge(z_hi_done, 1)
                nc.vector.tensor_tensor(zt[1][:].rearrange("p a b c -> p (a b c)"), side[:, 2, :],
                                        zt[0][:].rearrange("p a b c -> p (a b c)").bitcast(F32), ALU.subtract)\
                    .then_inc(z_lo_done, 1)

            def heads2(t):
                return t[:].rearrange("p r s t -> p r (s t)")

            strict2 = strict[:].rearrange("p s t -> p (s t)").unsqueeze(1).broadcast_to([P, 2, 2 * S])

            def stick_mask(u):
                dve.wait_ge(stick_soft, u + 1)
                dve.wait_ge(stick_loaded, 32)
                sp = heads2(stick_l[u])
                then(nc.vector.scalar_tensor_tensor(out=sp, in0=heads2(stick_z[u]), scalar=0.0, in1=sp,
                                                    op0=ALU.max, op1=ALU.add))
                nc.vector.tensor_tensor(sp, sp, strict2, ALU.mult).then_inc(stick_masked, 1)

            def stick_args(u):
                dve.wait_ge(stick_sums, u + 1)
                e2 = heads2(stick_e[u])
                then(nc.vector.tensor_tensor(e2, heads2(stick_z[u]), side[:, 2:4, :], ALU.add))
                nc.vector.tensor_scalar(e2, e2, 0.0, None, ALU.min).then_inc(stick_arg, 1)

            def stick_weigh(u):
                dve.wait_ge(stick_exp, u + 1)
                e2 = heads2(stick_e[u])
                nc.vector.tensor_tensor(e2, e2, strict2, ALU.mult).then_inc(stick_weights, 1)

            def stick_out_lo(u):
                dve.wait_ge(stick_hi, u + 1)
                nc.vector.tensor_tensor(ot["a"][1][:, :, 2 * u:2 * u + 2, :],
                                        side[:, 0, :].rearrange("p (r h t) -> p h r t", r=2, h=NT),
                                        ot["a"][0][:, :, 2 * u:2 * u + 2, :].bitcast(F32), ALU.subtract)\
                    .then_inc(stick_lo, 1)

            def merge(s, b, n):
                before = MERGE.index(b) * GRP + n
                if before == 0:
                    dve.wait_ge(pv_done, len(PASSES))
                dve.wait_ge(bank_free[1], GN_MIX // 2 + before + 1)
                dve.wait_ge(chunk_used, s - LEAD + 1)
                for h in range(NT):
                    dst = rows[:, h, n * 512:(n + 1) * 512] if b == MERGE[0] else gate[:, n % 2, h, :]
                    e = nc.vector.tensor_tensor(dst, acc[:, 0, h, :], gate[:, n % 2, h, :], ALU.mult)
                e.then_inc(bank_free[0], 1)
                dve.wait_ge(bank_free[0], (GN_MIX + 1) // 2 + before + 1)
                if b == MERGE[0]:
                    dve.nop().then_inc(gate_used, 1)
                else:
                    for h in range(NT):
                        dst = rows[:, h, n * 512:(n + 1) * 512]
                        e = nc.vector.tensor_tensor(dst, dst, gate[:, n % 2, h, :], ALU.add)
                    e.then_inc(gate_used, 1)

            def rows_lo(q):
                dve.wait_ge(xt_hi_done, KT + q + 1)
                k = 2 * (q % (KT // 2))
                if q < KT // 2:
                    e = nc.vector.tensor_tensor(flat(xt_lo[:, k:k + 2, :]), side[:, q % 4, :],
                                                flat(xt_hi[:, k:k + 2, :]).bitcast(F32), ALU.subtract)
                else:
                    for j in range(2):
                        hi, lo_ = ((x2_hi[:, k + j, :], x2_lo[:, k + j, :]) if k < NX2
                                   else (x3_hi[:, k + j - NX2, :], x3_lo[:, k + j - NX2, :]))
                        e = nc.vector.scalar_tensor_tensor(
                            out=lo_, in0=side[:, q % 4, j * S:(j + 1) * S], scalar=g_ffn[:, k + j:k + j + 1],
                            in1=hi.bitcast(F32), op0=ALU.mult, op1=ALU.subtract)
                e.then_inc(xt_lo_done, 1)

            def add_rows(g, ch0, parity, rows=rows):
                dve.wait_ge(chunk_used, g * CPG + (ch0 + CPG))
                for h in range(NT):
                    dst = rows[:, h, bass.ds(g * 512, 512)]
                    e = nc.vector.tensor_tensor(dst, acc[:, parity, h, :], dst, ALU.add)
                e.then_inc(bank_free[parity], 1)

            def rank_keys(r, h, side_i):
                if h == 0 and side_i == 0 and r % 4 == 0:
                    dve.wait_ge(act_copied, 2 * (r // 4) + 2)
                src = key_s[:, h, r, side_i, :]
                v, n = key_v[:, h, r, side_i, :], key_i[:, h, r, side_i, :]
                then(nc.vector.max(v[:, 0:8], src))
                nc.vector.max_index(n[:, 0:8], v[:, 0:8], src)
                then(nc.vector.match_replace(key_w[:], v[:, 0:8], src, TAKEN))
                then(nc.vector.max(v[:, 8:16], key_w[:]))
                then(nc.vector.max_index(n[:, 8:16], v[:, 8:16], key_w[:]))

            def pair_grid(r, h):
                v = key_v[:, h, r]
                then(nc.vector.tensor_tensor(cand[:], v[:, 0, :].unsqueeze(2).broadcast_to([P, PK, PK]),
                                             v[:, 1, :].unsqueeze(1).broadcast_to([P, PK, PK]), ALU.add))

            def rank_pairs(r, h, second):
                c = flat(cand[:])
                v, n = pair_v[:, h, r, 8 * second:8 * second + 8], pair_i[:, h, r, 8 * second:8 * second + 8]
                then(nc.vector.max(v, c))
                then(nc.vector.max_index(n, v, c))
                if not second:
                    then(nc.vector.match_replace(c, v, c, TAKEN))

            def place_pairs(r, h):
                n = pair_i[:, h, r, :]
                nc.vector.tensor_scalar(pair_n[:, 0, :], n, 4, None, ALU.logical_shift_right)
                then(nc.vector.tensor_scalar(pair_n[:, 1, :], n, 15, None, ALU.bitwise_and))
                nc.vector.tensor_copy(pair_f[:], pair_n[:])
                then(nc.vector.tensor_copy(key_f[:], key_i[:, h, r]))

            def look_up(r, h, side_i):
                if (r, h, side_i) == (0, 0, 0):
                    dve.wait_ge(iotas_loaded, 16)
                then(nc.vector.tensor_tensor(cand[:], pair_f[:, side_i, :].unsqueeze(2).broadcast_to([P, PK, PK]),
                                             iotas[:, 0:PK].unsqueeze(1).broadcast_to([P, PK, PK]), ALU.is_equal))
                then(nc.vector.tensor_tensor(cand[:], cand[:],
                                             key_f[:, side_i, :].unsqueeze(1).broadcast_to([P, PK, PK]), ALU.mult))
                then(nc.vector.tensor_reduce(picks[:, h, side_i, r, :], cand[:], AX, ALU.add))

            def split_place(r, h):
                then(nc.vector.tensor_copy(pick_n[:, 0, :], picks[:, h, 1, r, :]))
                then(nc.vector.tensor_scalar(pick_n[:, 1, :], pick_n[:, 0, :], 1, 6, ALU.bitwise_and,
                                             ALU.logical_shift_left))
                then(nc.vector.tensor_scalar(pick_n[:, 0, :], pick_n[:, 0, :], 1, None, ALU.logical_shift_right))
                then(nc.vector.tensor_copy(pair_f[:], pick_n[:]))
                nc.vector.tensor_copy(picks[:, h, 1, r, :], pair_f[:, 0, :])
                then(nc.vector.tensor_tensor(picks[:, h, 0, r, :], picks[:, h, 0, r, :], pair_f[:, 1, :], ALU.add))

            def rank(unit, step):
                r, h = unit // NT, unit % NT
                if step < 2:
                    rank_keys(r, h, step)
                elif step == 2:
                    pair_grid(r, h)
                    rank_pairs(r, h, 0)
                elif step == 3:
                    rank_pairs(r, h, 1)
                    place_pairs(r, h)
                    look_up(r, h, 0)
                else:
                    look_up(r, h, 1)
                    split_place(r, h)

            pv = pair_v[:].rearrange("p h r k -> p (h r) k")

            def shift_picks():
                then(nc.vector.tensor_copy(soft_inv, pv[:, :, 0]))
                nc.vector.tensor_tensor(pv, pv, soft_inv.unsqueeze(2).broadcast_to([P, NT * PH, PK]), ALU.subtract)\
                    .then_inc(picks_shifted, 1)

            def weigh_picks():
                dve.wait_ge(picks_exp, 1)
                then(nc.vector.tensor_reduce(soft_den, pv, AX, ALU.add))
                then(nc.vector.reciprocal(soft_inv, soft_den))
                for h in range(NT):
                    e = nc.vector.tensor_tensor(picks[:, h, 2], pair_v[:, h],
                                                soft_inv[:, h * PH:(h + 1) * PH].unsqueeze(2)
                                                .broadcast_to([P, PH, PK]), ALU.mult)
                e.then_inc(picks_ready, 1)

            def copy_picks():
                dve.wait_ge(picks_turned, 1)
                for h in range(NT):
                    e = nc.vector.tensor_copy(kmaj[:, :, tile_rows(h)],
                                              side[:, h, 0:3 * P].rearrange("p (c t) -> p c t", t=P))
                e.then_inc(picks_copied, 1)

            def one_hots(n):
                t = slice(n * HOT, (n + 1) * HOT)
                if n == 0:
                    dve.wait_ge(picks_copied, 1)
                if n >= 3:
                    dve.wait_ge(scattered, n - 2)
                then(nc.vector.tensor_tensor(hot_q[:, n % 3], kmaj[:, 1, t].unsqueeze(2).broadcast_to([P, HOT, 32]),
                                             iotas[:, 0:32].unsqueeze(1).broadcast_to([P, HOT, 32]), ALU.is_equal))
                nc.vector.tensor_tensor(hot_q[:, n % 3], hot_q[:, n % 3],
                                        kmaj[:, 2, t].unsqueeze(2).broadcast_to([P, HOT, 32]), ALU.mult)\
                    .then_inc(hot_q_ready, 1)
                if n % 2 == 0:
                    nc.vector.tensor_tensor(hot_c[n % 3][:], kmaj[:, 0, t].unsqueeze(2).broadcast_to([P, HOT, P]),
                                            iotas[:].unsqueeze(1).broadcast_to([P, HOT, P]), ALU.is_equal)\
                        .then_inc(hot_c_ready[0], 1)

            def weigh_act(q):
                if q == 0:
                    dve.wait_ge(gates_put, ROUNDS)
                dve.wait_ge(act_copied, 4 + q + 1)
                w = flat(wmat[:, 2 * q:2 * q + 2, :])
                nc.vector.tensor_tensor(w, w, flat(act_t[:, 2 * q:2 * q + 2, :]), ALU.mult).then_inc(wmat_ready, 1)

            def wmat_lo_part(q):
                dve.wait_ge(wmat_hi, q + 1)
                if q == 4:
                    dve.wait_ge(chunk_used, CH_V)
                if q == 12:
                    dve.wait_ge(act_turned, 2 * GRP)
                nc.vector.tensor_tensor(flat(xt_lo[:, 2 * q:2 * q + 2, :]), flat(wmat[:, 2 * q:2 * q + 2, :]),
                                        flat(xt_hi[:, 2 * q:2 * q + 2, :]).bitcast(F32), ALU.subtract)\
                    .then_inc(wmat_lo, 1)

            def between(s):
                for br, at_slot in NORM_AT.items():
                    i = s - at_slot
                    if 0 <= i < 8 * NORM_STEP[br] and i % NORM_STEP[br] == 0:
                        norm_piece(br, i // NORM_STEP[br])
                for h, at_slot in enumerate(INDEX_READ):
                    if s == at_slot:
                        read_index(h)
                    if at_slot < s <= at_slot + 4:
                        select(h, s == at_slot + 4)
                if s == INDEX_READ[0] + 6:
                    compressed_blocks()
                if s == CMP_OUT + LEAD:
                    cmp_squares()
                if s == CMP_OUT + LEAD + 2:
                    cmp_norm()
                if s == CMP_OUT + LEAD + 6:
                    cmp_copy()
                if s == Z_TURN + LEAD + 1:
                    z_lo()
                for i, at_slot in enumerate(PASS_AT):
                    if s == at_slot + 3:
                        mask_scores(i)
                    if s == at_slot + 6:
                        normalise(i)
                    if s == at_slot + 11 and last_part(PASSES[i][0], PASSES[i][2]):
                        out_lo(i)
                for u, at_slot in enumerate(STICK_AT):
                    if s == at_slot + 6:
                        stick_mask(u)
                    if s == at_slot + 12:
                        stick_args(u)
                    if s == at_slot + 15:
                        stick_weigh(u)
                    if s == at_slot + 20:
                        stick_out_lo(u)
                if s in MIX_OUT:
                    merge(s, *MIX_OUT[s])
                if s - LEAD - 1 in XT_TURN:
                    rows_lo(XT_TURN[s - LEAD - 1])
                if s in OUT_OUT:
                    if OUT_OUT[s] == 0:
                        dve.wait_ge(x_loaded, 16)
                    add_rows(OUT_OUT[s], CH_OUT, (GN_OUT + OUT_OUT[s]) % 2)
                if RANK_AT <= s < RANK_AT + 16 * RANK_STEP:
                    rank((s - RANK_AT) // RANK_STEP, (s - RANK_AT) % RANK_STEP)
                if s == SOFTMAX_AT:
                    shift_picks()
                if s == SOFTMAX_AT + 2:
                    weigh_picks()
                if s == PICKS_TURN + LEAD:
                    copy_picks()
                n = s - SCATTER_AT - 1
                if 0 <= n < ROUNDS:
                    one_hots(n)
                if 0 <= s - CH_V + 1 < KT // 2:
                    weigh_act(s - CH_V + 1)
                if 0 <= s - CH_V - 1 < KT // 2:
                    wmat_lo_part(s - CH_V - 1)
                if s == CH_V + CPG + LEAD:
                    dve.wait_ge(h_loaded, 16)
                    add_rows(0, CH_V, GN_V % 2, h_rows)

            nc.vector.memset(half_exp, -0.5).then_inc(half_ready, 1)
            dve.wait_ge(g_mix_loaded, 16)
            for k in range(KT):
                dve.wait_ge(xt_hi_done, k + 1)
                nc.vector.scalar_tensor_tensor(out=xt_lo[:, k, :], in0=xt_raw[:, k, :], scalar=g_mix[:, k:k + 1],
                                               in1=xt_hi[:, k, :].bitcast(F32), op0=ALU.mult, op1=ALU.subtract)\
                    .then_inc(xt_lo_done, 1)
                if k % 2 and k // 2 < RING:
                    lo(k // 2, k // 2, 2 * W1C)
            for s in range(RING, CH_V + 2 * CPG):
                if s not in SHARED_LO:
                    lo(s, s % RING, 2 * W1C if s < CH_MIX else 1024)
                between(s)
                if s in SHARED_LO:
                    dve.wait_ge(lo_shared, SHARED_LO.index(s) + 1)
                    dve.nop().then_inc(lo_ready, 1)
            with dve.Fori(1, GRP // 2) as m:
                for k in range(2):
                    los(m * (2 * CPG) + (CH_V + k * CPG), 0, 4)
                    add_rows(m * 2 + (k - 1), CH_V, (GN_V + k - 1) % 2, h_rows)
                    los(m * (2 * CPG) + (CH_V + k * CPG), 4, CPG)
            add_rows(GRP - 1, CH_V, (GN_V + GRP - 1) % 2, h_rows)

        @block.gpsimd
        def _(pool):
            then = chain(pool, pool_chain)

            def rsqrt_mean(out, total, n, parts=P):
                w = out.shape[1]
                then(nc.gpsimd.tensor_scalar(out, total, 1.0 / n, EPS, ALU.mult, ALU.add))
                return nc.gpsimd.tensor_tensor(out, out, half_exp[0:parts, 0:w], ALU.pow)

            def row_rstd(rstd, ms, squares):
                pool.wait_ge(squares_done, squares)
                halves = ms.rearrange("p (h a) -> p h a", a=2)
                then(nc.gpsimd.tensor_tensor(rstd, halves[:, :, 0], halves[:, :, 1], ALU.add))
                rsqrt_mean(rstd, rstd, D).then_inc(rstd_ready, 1)

            def branch_rstd(br):
                for h in range(NT):
                    pool.wait_ge(head_ms_done, "bcd".index(br) * NT + h + 1)
                    n = HEADS[br][2]
                    rsqrt_mean(head_rstd[br, h][:, 0:n], head_ms[br, h][:, 0:n], HD).then_inc(head_rstd_done, 1)

            pool.wait_ge(half_ready, 1)
            row_rstd(rstd_x, ms_x, 4)
            branch_rstd("b")
            branch_rstd("c")
            pool.wait_ge(cmp_square, 1)
            rsqrt_mean(k_rstd, k_ms, HD, NCMP).then_inc(cmp_rstd, 1)
            branch_rstd("d")
            pool.wait_ge(chunk_used, CH_MIX)
            pool.dma_start(strict[:], io["strict"]).then_inc(stick_loaded, 16)
            pool.dma_start(tri[:], io["tri"]).then_inc(stick_loaded, 16)
            pool.wait_ge(gate_used, len(MERGE) * GRP)
            pool.dma_start(iotas[:], io["iotas"]).then_inc(iotas_loaded, 16)
            pool.wait_ge(xt_turned, KT // 2)
            pool.dma_start(rows[:], io["x"]).then_inc(x_loaded, 16)
            pool.wait_ge(chunk_used, CH_WQ)
            pool.dma_start(subkeys[:], io["subkeys"]).then_inc(subkeys_loaded, 16)
            row_rstd(rstd_h, ms_h, 8)
            evacuated(pool, GN_WQ - 1)
            for h in range(NT):
                pool.wait_ge(chunk_used, CH_WQ + CPG * (h + 1))
                pool.dma_start(io["h"][:, h, :], rows[:, h, :]).then_inc(h_stored, 16)
            for s in SHARED_LO:
                pool.wait_ge(hi_ready, s + 1)
                nc.gpsimd.tensor_tensor(w_lo[:, s % RING, :], w_raw[:, s % RING, :],
                                        w_hi[:, s % RING, :].bitcast(F32), ALU.subtract).then_inc(lo_shared, 1)
            pool.wait_ge(picks_copied, 1)
            pool.wait_ge(iotas_loaded, 16)
            for n in range(1, ROUNDS, 2):
                if n >= 3:
                    pool.wait_ge(scattered, n - 2)
                nc.gpsimd.tensor_tensor(hot_c[n % 3][:],
                                        kmaj[:, 0, n * HOT:(n + 1) * HOT].unsqueeze(2).broadcast_to([P, HOT, P]),
                                        iotas[:].unsqueeze(1).broadcast_to([P, HOT, P]), ALU.subtract)\
                    .then_inc(hot_distance, 1)
            pool.wait_ge(chunk_used, CH_V)
            pool.wait_ge(h_stored, 32)
            pool.dma_start(h_rows[:], io["h"]).then_inc(h_loaded, 16)
            pool.wait_ge(h_loaded, 16)
            with pool.Fori(0, GRP // 2) as m:
                for k in range(2):
                    gn = GN_V + k
                    pool.wait_ge(bank_free[gn % 2], m + (gn // 2 + 1))
                    pool.dma_start(io["out"][:, :, bass.ds(m * 1024 + k * 512, 512)],
                                   h_rows[:, :, bass.ds(m * 1024 + k * 512, 512)]).then_inc(stored, 16)
            pool.wait_ge(stored, 16 * GRP)


def tiles(w, width):
    k, n = w.shape
    return (w.reshape(k // 256, 2, P, n // width, width).transpose(3, 0, 2, 1, 4)
            .reshape(n // width, k // 256, P, 2 * width))


def kernel(x, norm_mix, w_in, qk_gain, nsa_pe, nsa_w1, nsa_w2, gate_down, gate_up, w_branch, w_out,
           norm_ffn, peer_wq, peer_subkeys, peer_u, peer_v):
    import concourse.bacc as bacc
    from concourse.bass_utils import run_bass_kernel_spmd

    arr = {k: np.asarray(v) for k, v in dict(
        x=x, norm_mix=norm_mix, w_in=w_in, qk_gain=qk_gain, nsa_pe=nsa_pe, nsa_w1=nsa_w1, nsa_w2=nsa_w2,
        gate_down=gate_down, gate_up=gate_up, w_branch=w_branch, w_out=w_out, norm_ffn=norm_ffn,
        peer_wq=peer_wq, peer_subkeys=peer_subkeys, peer_u=peer_u, peer_v=peer_v).items()}
    f = np.float32
    widths = (512, 512, 512, 512, 128, 128, 256, 64, 4, 512, 128, 128, 128, 128, 128, 128, 12, 768, 256, 256)
    names = ("aq", "ak", "av", "bq", "bk", "bv", "biq", "bik", "biw", "cq", "ckc", "cvc", "cks", "cvs", "ckw", "cvw",
             "cg", "dq", "dk", "dv")
    col = dict(zip(names, np.split(arr["w_in"][0], np.cumsum(widths)[:-1], axis=1)))
    w1 = np.concatenate([col[n] for n in ("bq", "bk", "ckc", "biq", "bik", "biw", "cg", "cvc", "bv",
                                          "cq", "cks", "ckw", "cvs", "cvw", "dq", "dk", "dv")]
                        + [arr["gate_down"][0]] + [col[n] for n in ("aq", "ak", "av")], axis=1)
    wb = np.split(arr["w_branch"][0], (512, 1024, 1536), axis=0)
    parts = []
    for b in (1, 2, 3, 0):
        gu, w = tiles(arr["gate_up"][0, b], 512), tiles(wb[b], 512)
        parts.append(np.concatenate([gu, w], axis=1).reshape(-1, P, 1024))
    parts.append(tiles(arr["w_out"][0], 512).reshape(-1, P, 1024))
    parts.append(tiles(arr["peer_wq"][0], 512).reshape(-1, P, 1024))
    order = lambda w: w.reshape(64, 32, 2, D).transpose(1, 2, 0, 3).reshape(D, D)
    parts.append(tiles(order(arr["peer_u"][0]).T, 512).reshape(-1, P, 1024))
    parts.append(tiles(order(arr["peer_v"][0]), 512).reshape(-1, P, 1024))
    stream = np.concatenate(parts, axis=0)
    sk = np.zeros((P, PH, P), f)
    for b in range(2):
        sk[64 * b:64 * b + 64, :, 64 * b:64 * b + 64] = arr["peer_subkeys"][0, :, b].transpose(2, 0, 1)

    t = np.arange(S)
    d = t[:, None] - t[None, :]
    by_tile = lambda m: np.ascontiguousarray(m.reshape((NT, P) + m.shape[1:]).swapaxes(0, 1), dtype=f)
    keep = lambda m: np.where(m, 0.0, NEG).astype(f)
    dil = np.stack([keep((d >= 0) & (d <= w) & (d % r == 0)) for w, r in ((128, 1), (512, 4), (2048, 16))], axis=1)
    inv = f(10000.0) ** (-np.arange(0, HD, 2, dtype=f) / f(HD))
    ang = (t.astype(f)[:, None] * inv[None, :]).astype(f)
    rope = np.stack([by_tile(np.cos(ang)), by_tile(np.sin(ang)), by_tile(-np.sin(ang))], axis=1)
    k = np.arange(P)
    host = {
        "w_in": tiles(w1, W1C).reshape(-1, P, 2 * W1C),
        "stream": stream,
        "xt": arr["x"][0].T.reshape(KT, P, S).transpose(1, 0, 2),
        "x": arr["x"][0].reshape(NT, P, D).transpose(1, 0, 2),
        "g_mix": arr["norm_mix"][0].reshape(KT, P).T,
        "g_ffn": arr["norm_ffn"][0].reshape(KT, P).T,
        "gains": arr["qk_gain"][0].reshape(1, 8, HD),
        "cmp_w1": arr["nsa_w1"][0].transpose(0, 2, 1, 3),
        "cmp_w2": arr["nsa_w2"][0].transpose(1, 0, 2),
        "pe_t": arr["nsa_pe"][0].transpose(2, 0, 1),
        "subkeys": sk,
        "ident": np.eye(P, dtype=f),
        "iotas": np.broadcast_to(np.arange(P, dtype=f), (P, P)),
        "causal": by_tile(keep(d >= 0)),
        "dil": by_tile(dil),
        "strict": by_tile((d > 0).T.astype(f)),
        "rope": rope,
        "tri": np.stack([-(k[:, None] >= k[None, :]).astype(f), -np.ones((P, P), f)], axis=1),
        "cmp_mask": by_tile(keep(t[:, None] >= 16 * np.arange(NCMP)[None, :] + 31)),
    }
    host = {n: np.ascontiguousarray(a) for n, a in host.items()}
    nc = bacc.Bacc("TRN2", target_bir_lowering=False, num_devices=1)
    io, maps = {}, {}
    for n, a in host.items():
        io[n] = nc.dram_tensor("in_" + n, a.shape, F32, kind="ExternalInput").ap()
        maps["in_" + n] = a
    out = nc.dram_tensor("out_h", (1, S, D), F32, kind="ExternalOutput").ap()
    io["h"] = nc.dram_tensor("h_rows_d", (P, NT, D), F32, kind="Internal").ap()
    io["out"] = out.rearrange("a (h p) d -> p (a h) d", p=P)
    io["gains"] = io["gains"].rearrange("a g d -> a (g d)").broadcast_to([P, 8 * HD]).rearrange("p (g d) -> p g d", d=HD)
    build(nc, io)
    r = run_bass_kernel_spmd(nc, [maps], core_ids=[0])
    return r.results[0]["out_h"]
```
